# Optimizing a Trainium2 kernel written in Bass

```python
import jax, jax.numpy as jnp
from jax import lax
import numpy as np

D_MODEL = 2048
BATCH = 1
SEQ = 256
DEPTH = 1

N_HEADS = 16
HEAD_DIM = 128
ATTN_WIDTH = N_HEADS * HEAD_DIM
MOBA_BLOCK = 256
MOBA_TOPK = 3
Q_CHUNK = 64
CONV_WIDTH = 1024
CONV_KERNEL = 31
D_FF = 5632
LN_EPS = 1e-5
DN_ALPHA = (2 * DEPTH) ** 0.25
DN_BETA = (8 * DEPTH) ** -0.25
IN_SPLITS = [ATTN_WIDTH, ATTN_WIDTH, ATTN_WIDTH, 2 * CONV_WIDTH, D_MODEL, D_MODEL]
IN_COLS = sum(IN_SPLITS)

kernel_name = "moba_conformer_gated_hybrid_deepnorm"

def alibi_slopes():
    return jnp.asarray(np.array([2.0 ** (-8.0 * (h + 1) / N_HEADS) for h in range(N_HEADS)], dtype=np.float32))

def layer_norm(x, g, b):
    xf = x.astype(jnp.float32)
    mu = jnp.mean(xf, -1, keepdims=True)
    var = jnp.mean(jnp.square(xf - mu), -1, keepdims=True)
    return ((xf - mu) * lax.rsqrt(var + LN_EPS)).astype(x.dtype) * g + b

def swiglu(x, wg, wu, wd):
    return (jax.nn.silu(x @ wg) * (x @ wu)) @ wd

def moba_attention(q, k, v):
    B, H, S, Dh = q.shape
    L = MOBA_BLOCK
    nb = -(-S // L)
    pad = ((0, 0), (0, 0), (0, nb * L - S), (0, 0))
    kp = jnp.pad(k, pad)
    vp = jnp.pad(v, pad)
    k_blk = kp.reshape(B, H, nb, L, Dh)
    v_blk = vp.reshape(B, H, nb, L, Dh)
    k_mean = jnp.mean(k_blk.astype(jnp.float32), axis=3)
    q_blk = jnp.arange(S) // L
    gate = jnp.einsum('bhsd,bhnd->bhsn', q.astype(jnp.float32), k_mean)
    past = jnp.arange(nb)[None, :] < q_blk[:, None]
    gate = jnp.where(past, gate, -jnp.inf)
    n_sel = min(MOBA_TOPK, nb)
    _, sel_idx = lax.top_k(gate, n_sel)
    sel_valid = jnp.arange(n_sel)[None, :] < q_blk[:, None]

    scale = HEAD_DIM ** -0.5
    slopes = alibi_slopes()
    sl4 = slopes.reshape(1, H, 1, 1)
    sl5 = slopes.reshape(1, H, 1, 1, 1)
    bi = jnp.arange(B)[:, None, None, None]
    hi = jnp.arange(H)[None, :, None, None]

    def chunk(c):
        t0 = c * Q_CHUNK
        t = t0 + jnp.arange(Q_CHUNK)
        q_c = lax.dynamic_slice_in_dim(q, t0, Q_CHUNK, axis=2)
        idx_c = lax.dynamic_slice_in_dim(sel_idx, t0, Q_CHUNK, axis=2)
        val_c = lax.dynamic_slice_in_dim(sel_valid, t0, Q_CHUNK, axis=0)
        k_sel = k_blk[bi, hi, idx_c]
        v_sel = v_blk[bi, hi, idx_c]
        s_sel = idx_c[..., None] * L + jnp.arange(L)
        sc_sel = jnp.einsum('bhqd,bhqnld->bhqnl', q_c, k_sel).astype(jnp.float32) * scale
        sc_sel = sc_sel - sl5 * (t[:, None, None] - s_sel).astype(jnp.float32)
        sc_sel = jnp.where(val_c[:, :, None], sc_sel, -jnp.inf)
        own0 = (t0 // L) * L
        k_own = lax.dynamic_slice_in_dim(kp, own0, L, axis=2)
        v_own = lax.dynamic_slice_in_dim(vp, own0, L, axis=2)
        s_own = own0 + jnp.arange(L)
        sc_own = jnp.einsum('bhqd,bhld->bhql', q_c, k_own).astype(jnp.float32) * scale
        sc_own = sc_own - sl4 * (t[:, None] - s_own[None, :]).astype(jnp.float32)
        sc_own = jnp.where(s_own[None, :] <= t[:, None], sc_own, -jnp.inf)
        scores = jnp.concatenate([sc_sel.reshape(B, H, Q_CHUNK, n_sel * L), sc_own], axis=-1)
        p = jax.nn.softmax(scores, axis=-1)
        p_sel = p[..., :n_sel * L].reshape(B, H, Q_CHUNK, n_sel, L).astype(v.dtype)
        p_own = p[..., n_sel * L:].astype(v.dtype)
        return (jnp.einsum('bhqnl,bhqnld->bhqd', p_sel, v_sel)
                + jnp.einsum('bhql,bhld->bhqd', p_own, v_own))

    outs = lax.map(chunk, jnp.arange(S // Q_CHUNK))
    return outs.transpose(1, 2, 0, 3, 4).reshape(B, H, S, Dh)

def conformer_conv(u, w_dw, b_dw, ln_g, ln_b, w_pw2):
    a, g = jnp.split(u, 2, axis=-1)
    h = a * jax.nn.sigmoid(g)
    h = lax.conv_general_dilated(h, w_dw, window_strides=(1,), padding=[(CONV_KERNEL - 1, 0)],
                                 dimension_numbers=('NWC', 'WIO', 'NWC'),
                                 feature_group_count=CONV_WIDTH) + b_dw
    h = jax.nn.silu(layer_norm(h, ln_g, ln_b))
    return h @ w_pw2

def token_mixer(h, w_in, conv_dw, conv_db, conv_ln_g, conv_ln_b, w_conv_out, w_attn_out, w_out):
    B, S, _ = h.shape
    z = h @ w_in
    q, k, v, u, ga, gc = jnp.split(z, list(np.cumsum(IN_SPLITS)[:-1]), axis=-1)
    to_heads = lambda t: t.reshape(B, S, N_HEADS, HEAD_DIM).transpose(0, 2, 1, 3)
    o = moba_attention(to_heads(q), to_heads(k), to_heads(v))
    y_attn = o.transpose(0, 2, 1, 3).reshape(B, S, ATTN_WIDTH) @ w_attn_out
    y_conv = conformer_conv(u, conv_dw, conv_db, conv_ln_g, conv_ln_b, w_conv_out)
    merged = jax.nn.sigmoid(ga) * y_attn + jax.nn.sigmoid(gc) * y_conv
    return merged @ w_out

def setup_inputs(seed: int = 0) -> dict:
    key = jax.random.key(seed)
    ks = jax.random.split(key, 24)
    f32 = jnp.float32
    nrm = lambda k, shape, s: jax.random.normal(k, shape, f32) * s
    gain = lambda k, n: 1.0 + nrm(k, (DEPTH, n), 0.02)
    bias = lambda k, n: nrm(k, (DEPTH, n), 0.02)
    return {
        "x": jax.random.normal(ks[0], (BATCH, SEQ, D_MODEL), f32),
        "ln1_g": gain(ks[1], D_MODEL), "ln1_b": bias(ks[2], D_MODEL),
        "ffn1_wg": nrm(ks[3], (DEPTH, D_MODEL, D_FF), D_MODEL ** -0.5),
        "ffn1_wu": nrm(ks[4], (DEPTH, D_MODEL, D_FF), D_MODEL ** -0.5),
        "ffn1_wd": nrm(ks[5], (DEPTH, D_FF, D_MODEL), DN_BETA * D_FF ** -0.5),
        "w_in": nrm(ks[6], (DEPTH, D_MODEL, IN_COLS), D_MODEL ** -0.5),
        "conv_dw": nrm(ks[7], (DEPTH, CONV_KERNEL, 1, CONV_WIDTH), CONV_KERNEL ** -0.5),
        "conv_db": bias(ks[8], CONV_WIDTH),
        "conv_ln_g": gain(ks[9], CONV_WIDTH), "conv_ln_b": bias(ks[10], CONV_WIDTH),
        "w_conv_out": nrm(ks[11], (DEPTH, CONV_WIDTH, D_MODEL), DN_BETA * CONV_WIDTH ** -0.5),
        "w_attn_out": nrm(ks[12], (DEPTH, ATTN_WIDTH, D_MODEL), DN_BETA * ATTN_WIDTH ** -0.5),
        "w_out": nrm(ks[13], (DEPTH, D_MODEL, D_MODEL), DN_BETA * D_MODEL ** -0.5),
        "ln2_g": gain(ks[14], D_MODEL), "ln2_b": bias(ks[15], D_MODEL),
        "ffn2_wg": nrm(ks[16], (DEPTH, D_MODEL, D_FF), D_MODEL ** -0.5),
        "ffn2_wu": nrm(ks[17], (DEPTH, D_MODEL, D_FF), D_MODEL ** -0.5),
        "ffn2_wd": nrm(ks[18], (DEPTH, D_FF, D_MODEL), DN_BETA * D_FF ** -0.5),
        "ln3_g": gain(ks[19], D_MODEL), "ln3_b": bias(ks[20], D_MODEL),
    }

def reference(x, ln1_g, ln1_b, ffn1_wg, ffn1_wu, ffn1_wd, w_in, conv_dw, conv_db, conv_ln_g, conv_ln_b,
              w_conv_out, w_attn_out, w_out, ln2_g, ln2_b, ffn2_wg, ffn2_wu, ffn2_wd, ln3_g, ln3_b):
    h = x
    for l in range(DEPTH):
        h = layer_norm(DN_ALPHA * h + 0.5 * swiglu(h, ffn1_wg[l], ffn1_wu[l], ffn1_wd[l]), ln1_g[l], ln1_b[l])
        mix = token_mixer(h, w_in[l], conv_dw[l], conv_db[l], conv_ln_g[l], conv_ln_b[l],
                          w_conv_out[l], w_attn_out[l], w_out[l])
        h = layer_norm(DN_ALPHA * h + mix, ln2_g[l], ln2_b[l])
        h = layer_norm(DN_ALPHA * h + 0.5 * swiglu(h, ffn2_wg[l], ffn2_wu[l], ffn2_wd[l]), ln3_g[l], ln3_b[l])
    return h


_drawn_inputs = setup_inputs


def setup_inputs(seed=0):
    import zlib

    import numpy as np

    out = dict(_drawn_inputs(seed))
    spreads = {}
    factors = {'ln1_g': 2.681,
     'ln1_b': 2.69,
     'conv_db': 8.0,
     'conv_ln_g': 160.699,
     'conv_ln_b': 168.867,
     'ln2_g': 2.757,
     'ln2_b': 2.718,
     'ln3_g': 24.644,
     'ln3_b': 24.365}
    for name, (base, spread) in spreads.items():
        noise = np.random.default_rng([zlib.crc32(name.encode()), seed]).standard_normal(out[name].shape)
        drawn = base * np.exp(spread * noise) if base else spread * noise
        out[name] = __import__('jax').numpy.asarray(drawn.astype(out[name].dtype))
    for name, factor in factors.items():
        out[name] = (out[name] * factor).astype(out[name].dtype)
    return out
```

```python
from contextlib import ExitStack

import numpy as np

import concourse.bass as bass
from concourse import mybir

F32 = mybir.dt.float32
F32R = mybir.dt.float32r
ACT = mybir.ActivationFunctionType
ALU = mybir.AluOpType
AX_X = mybir.AxisListType.X

P = 128
D = 2048
T = 256
TT = T // P
FF = 5632
H = 16
DH = 128
CC = 1024
TAPS = 31
PAD = TAPS - 1
EPS = 1e-5
ALPHA = 2.0 ** 0.25
SCALE = DH ** -0.5
COLS = 512
UK = 2
UNIT = UK * COLS
RAW = 4
SPLIT = 8
GROUP = 4

KD = D // P
UD = KD // UK
KF = FF // P
UF = KF // UK
KC = CC // P
UC = KC // UK
NFF = FF // COLS
ND = D // COLS
BLK = COLS // P
HG = 4
NG = H // HG
SC = 3 * P


class Segment:

    def __init__(self, before, n, chunks, iters):
        self.n, self.chunks, self.iters = n, chunks, iters
        if before is None:
            self.unit0, self.chunk0, self.raw0, self.split0, self.loads0 = 0, 0, 0, 0, [0] * RAW
        else:
            b = before
            self.unit0 = b.unit0 + b.n * b.iters
            self.chunk0 = b.chunk0 + b.chunks * b.iters
            self.raw0, self.split0 = (b.raw0 + b.n) % RAW, (b.split0 + b.n) % SPLIT
            self.loads0 = [x + y * b.iters for x, y in zip(b.loads0, b.loads_per_iteration())]

    def loads_per_iteration(self):
        return [sum(self.raw(j) == s for j in range(self.n)) for s in range(RAW)]

    def raw(self, j):
        return (self.raw0 + j) % RAW

    def split(self, j):
        return (self.split0 + j) % SPLIT

    def unit(self, i, j):
        return self.n * i + (self.unit0 + j)

    def loaded(self, i, j):
        s = self.raw(j)
        earlier = sum(self.raw(k) == s for k in range(j))
        return 16 * self.loads_per_iteration()[s] * i + 16 * (self.loads0[s] + earlier + 1)

    def before(self, i, j, slots):
        back = slots
        if self.n % slots and not (isinstance(i, int) and i == 0):
            back = self.n % slots if j < self.n % slots else self.n % slots + slots
            if j >= slots:
                back = slots
        v = self.unit(i, j) + 1 - back
        return None if isinstance(v, int) and v <= 0 else v

    def chunk(self, i, c):
        return self.chunks * i + (self.chunk0 + c)


def segments():
    up1 = Segment(None, 2 * UD, 2, NFF)
    down1 = Segment(up1, UF, 1, ND)
    conv_in = Segment(down1, 4 * UD, 4, 1)
    first_q = Segment(conv_in, UD, 1, 1)
    heads = Segment(first_q, 4 * UD, 4, NG)
    gates = Segment(heads, UD, 1, ND - 1)
    attn_out = Segment(gates, UD, 1, ND)
    conv_out = Segment(attn_out, ND * UC, ND, 1)
    mix_out = Segment(conv_out, UD, 1, ND)
    up2 = Segment(mix_out, 2 * UD, 2, NFF)
    down2 = Segment(up2, UF, 1, ND)
    return up1, down1, conv_in, first_q, heads, gates, attn_out, conv_out, mix_out, up2, down2


def build(nc, stream, xT, x, ln, conv_ln, conv_w, conv_b, consts, out):
    up1, down1, conv_in, first_q, heads, gates, attn_out, conv_out, mix_out, up2, down2 = segments()

    ctx = ExitStack()
    with ctx:
        base = -(-nc.sbuf_base // 64) * 64
        top = [base]

        def place(name, shape, dt=F32, at=None):
            size = 4 * int(np.prod(shape[1:]))
            if at is None:
                at = top[0]
                top[0] += -(-size // 32) * 32
            return nc.alloc_sbuf_tensor_at(name, shape, dt, offset=at)

        raw = place("raw", [P, RAW, UNIT])
        w_hi = place("w_hi", [P, SPLIT, UNIT], F32R)
        w_lo = place("w_lo", [P, SPLIT, UNIT], F32R)
        res = place("res", [P, TT, D])
        x_at = top[0]
        xT_hi = place("xT_hi", [P, KD, T], F32R)
        xT_lo = place("xT_lo", [P, KD, T], F32R)
        hid_at = top[0]
        hT_hi = place("hT_hi", [P, KF, T], F32R)
        hT_lo = place("hT_lo", [P, KF, T], F32R)
        hid_end = top[0]
        act_sb = place("act_sb", [P, TT, COLS])
        ident = place("ident", [P, P])
        stats = place("stats", [P, TT, ND, 6])
        mv = place("mv", [P, TT, 2])
        var_eps = place("var_eps", [P, TT, 1])
        rstd = place("rstd", [P, TT, 1])
        minus_half = place("minus_half", [P, 1])
        smax = place("smax", [P, 2 * HG])
        nmax = place("nmax", [P, 2 * HG])
        ssum = place("ssum", [P, 2 * HG])
        rsum = place("rsum", [P, 2 * HG])
        assert top[0] <= nc.sbuf_usable_end, (top[0], nc.sbuf_usable_end)
        x_stage = place("x_stage", [P, KD, T], at=hid_at)
        ln_gb = {0: place("ln1_gb", [P, 2, D], at=hid_at)}
        ln_gb[2] = ln_gb[0]
        at = [hid_at]

        def mix(name, shape, dt=F32):
            t = place(name, shape, dt, at=at[0])
            at[0] += 4 * int(np.prod(shape[1:]))
            return t

        sig = mix("sig", [P, 2 * ND, TT, COLS])
        oT_hi = mix("oT_hi", [P, H, T], F32R)
        oT_lo = mix("oT_lo", [P, H, T], F32R)
        qT = mix("qT", [P, HG, T])
        kT = mix("kT", [P, HG, T])
        vt = mix("vt", [P, TT, COLS])
        ch = mix("ch", [P, KC, PAD + T])
        alibi = mix("alibi", [P, SC + H])
        cw = mix("cw", [P, KC * TAPS + KC])
        assert at[0] <= hid_end
        gc_at = hid_at + 4 * ND * TT * COLS
        pr = place("pr", [P, HG, SC], at=gc_at)
        pT = place("pT", [P, HG, SC], at=gc_at + 4 * HG * SC)
        cacc = place("cacc", [P, 2, T], at=gc_at + 8 * HG * SC)
        ln_gb[1] = place("ln2_gb", [P, 2, D], at=gc_at)
        cT_hi = place("cT_hi", [P, KC, T], F32R, at=x_at)
        cT_lo = place("cT_lo", [P, KC, T], F32R, at=x_at + 4 * KC * T)
        ct = place("ct", [P, TT, CC], at=x_at + 8 * KC * T)
        cgb = place("cgb", [P, 2, CC], at=x_at + 8 * KC * T + 4 * TT * CC)

        acc = ctx.enter_context(nc.psum_tensor("acc", [P, 4, COLS], F32))
        tb = ctx.enter_context(nc.psum_tensor("tb", [P, 4, COLS], F32))

        def sem(name):
            return ctx.enter_context(nc.semaphore(name))

        raw_loaded = [sem(f"raw_loaded{s}") for s in range(RAW)]
        hi_ready = sem("hi_ready")
        lo_ready = sem("lo_ready")
        unit_used = sem("unit_used")
        tile0_full = sem("tile0_full")
        acc_out = [sem("acc_out0"), sem("acc_out1")]
        tr_full = sem("tr_full")
        lhs_hi = sem("lhs_hi")
        lhs_lo = sem("lhs_lo")
        x_loaded = [sem(f"x_loaded{s}") for s in range(4)]
        res_loaded = sem("res_loaded")
        ident_loaded = sem("ident_loaded")
        gb_loaded = sem("gb_loaded")
        cgb_loaded = sem("cgb_loaded")
        alibi_loaded = sem("alibi_loaded")
        cw_loaded = sem("cw_loaded")
        half_ready = sem("half_ready")
        ln_step = sem("ln_step")
        var_ready = sem("var_ready")
        rstd_ready = sem("rstd_ready")
        ln_ready = sem("ln_ready")
        ch_ready = sem("ch_ready")
        conv_step = sem("conv_step")
        qk_ready = sem("qk_ready")
        s_ready = sem("s_ready")
        smax_ready = sem("smax_ready")
        exp_ready = sem("exp_ready")
        p_ready = sem("p_ready")
        pT_ready = sem("pT_ready")
        silu_ready = sem("silu_ready")
        gated = sem("gated")
        merged = sem("merged")
        stored = sem("stored")

        u0_down1 = NFF
        u0_conv = u0_down1 + ND
        u0_q = u0_conv + 2
        u0_heads = u0_q + 1
        u1_heads = NFF + 2
        u0_gates = u0_heads + 2 * NG
        u1_attn = u1_heads + 2 * NG
        u0_convo = u0_gates + ND - 1
        u0_mix = u0_convo + ND
        u0_up2 = u0_mix + ND
        u1_up2 = u1_attn + ND
        u0_down2 = u0_up2 + NFF
        b_up1 = 4
        b_ln1 = b_up1 + 2 * NFF
        b_heads = b_ln1 + 8
        b_convt = b_heads + 2 * NG
        b_merge = b_convt + 4
        b_ln2 = b_merge + 2 * ND
        b_up2 = b_ln2 + 8
        t_up1 = 0
        t_ln1 = 2 * NFF
        t_conv = t_ln1 + 8
        t_heads = t_conv + 4
        TH = 2 + 2 + HG + HG + 2
        t_convo = t_heads + TH * NG
        t_convt = t_convo + 4
        t_merge = t_convt + 4
        t_ln2 = t_merge + 2 * ND
        t_up2 = t_ln2 + 8

        def f32(ap):
            return ap.bitcast(F32)

        block = ctx.enter_context(nc.Block())

        @block.sync
        def _(sp):
            def load(seg, i, j):
                v = seg.before(i, j, RAW)
                if v is not None:
                    sp.wait_ge(lo_ready, v)
                src = stream[bass.ds(seg.unit(i, j), 1)].rearrange("a p n -> p (a n)")
                sp.dma_start(raw[:, seg.raw(j)], src).then_inc(raw_loaded[seg.raw(j)], 16)

            def loads(seg, first=0):
                with sp.Fori(first, seg.iters) as i:
                    for j in range(seg.n):
                        load(seg, i, j)

            def load_once(seg):
                for j in range(seg.n):
                    load(seg, 0, j)

            def load_gb(n, dst):
                for k in range(2):
                    sp.dma_start(dst[:, k], ln[2 * n + k:2 * n + k + 1].to_broadcast([P, D])).then_inc(gb_loaded, 16)

            for j in range(up1.n):
                if j < 4:
                    sp.dma_start(x_stage[:, 4 * j:4 * j + 4], xT[:, 4 * j:4 * j + 4]).then_inc(x_loaded[j], 16)
                load(up1, 0, j)
                if j == 5:
                    sp.dma_start(ident[:], consts[:, 0:P]).then_inc(ident_loaded, 16)
                if j == 9:
                    sp.dma_start(res[:], x).then_inc(res_loaded, 16)
            loads(up1, 1)
            load_once(down1)
            loads(down1, 1)
            sp.wait_ge(unit_used, down1.unit(ND - 1, UD))
            load_gb(0, ln_gb[0])
            load_once(conv_in)
            load_once(first_q)
            sp.dma_start(alibi[:], consts[:, P:P + SC + H]).then_inc(alibi_loaded, 16)
            sp.dma_start(cw[:, 0:KC * TAPS], conv_w).then_inc(cw_loaded, 16)
            sp.dma_start(cw[:, KC * TAPS:], conv_b).then_inc(cw_loaded, 16)
            loads(heads)
            loads(gates)
            for j in range(attn_out.n):
                load(attn_out, 0, j)
            sp.wait_ge(unit_used, attn_out.unit(0, 0))
            for k in range(2):
                sp.dma_start(cgb[:, k], conv_ln[k:k + 1].to_broadcast([P, CC])).then_inc(cgb_loaded, 16)
            loads(attn_out, 1)
            load_once(conv_out)
            load_once(mix_out)
            sp.wait_ge(merged, 2 * ND)
            load_gb(1, ln_gb[1])
            loads(mix_out, 1)
            loads(up2)
            load_once(down2)
            loads(down2, 1)
            sp.wait_ge(unit_used, down2.unit(ND - 1, UD))
            load_gb(2, ln_gb[2])
            for n, (t, p) in enumerate((t, p) for t in range(TT) for p in range(ND)):
                sp.wait_ge(ln_ready, 18 + n + 1)
                cols = slice(p * COLS, (p + 1) * COLS)
                sp.dma_start(out[t * P:(t + 1) * P, cols], res[:, t, cols]).then_inc(stored, 16)
            sp.wait_ge(stored, 16 * TT * ND)

        @block.scalar
        def _(act):
            def hi(seg, i, *units):
                for j in units:
                    v = seg.before(i, j, SPLIT)
                    if v is not None:
                        act.wait_ge(unit_used, v)
                    act.wait_ge(raw_loaded[seg.raw(j)], seg.loaded(i, j))
                    act.activation(w_hi[:, seg.split(j)], raw[:, seg.raw(j)], ACT.Copy).then_inc(hi_ready, 1)

            def tile_full(seg, i, c, last, t):
                if t == 0:
                    act.wait_ge(tile0_full, seg.chunk(i, c) + 1)
                else:
                    act.wait_ge(unit_used, seg.unit(i, last) + 1)

            def block_hi(dst, bank, filled):
                act.wait_ge(tr_full, filled)
                act.activation(dst, tb[:, bank].rearrange("p (b n) -> p b n", b=BLK), ACT.Copy).then_inc(lhs_hi, 1)

            def gate(seg, i, func):
                for t in range(TT):
                    tile_full(seg, i, 0, UD - 1, t)
                    act.activation(act_sb[:, t], acc[:, t], func).then_inc(acc_out[0], 1)

            def norm_hi(t, pieces, filled):
                for p in pieces:
                    block_hi(xT_hi[:, BLK * p:BLK * (p + 1), t * P:(t + 1) * P], 2 * t + p % 2, filled)
                    filled += 1

            def after_norm(seg, t0):
                hi(seg, 0, 0, 1, 2, 3)
                norm_hi(0, (0, 1), t0 + 1)
                norm_hi(1, (0, 1), t0 + 3)
                norm_hi(0, (2, 3), t0 + 5)
                hi(seg, 0, 4, 5, 6, 7)
                norm_hi(1, (2, 3), t0 + 7)

            def hidden_hi(i, t0):
                for t in range(TT):
                    block_hi(hT_hi[:, bass.ds(BLK * i, BLK), t * P:(t + 1) * P], t, 2 * i + (t0 + t + 1))

            def up(seg, i, t0, start):
                if start is None:
                    hi(seg, i, 0, 1, 2, 3, 4, 5, 6, 7)
                    hidden_hi(i - 1, t0)
                else:
                    start()
                hi(seg, i, 8, 9, 10, 11)
                gate(seg, i, ACT.Silu)
                hi(seg, i, 12, 13, 14, 15)

            def down(seg, t0):
                hi(seg, 0, *range(8))
                hidden_hi(NFF - 1, t0)
                hi(seg, 0, *range(8, UF))
                with act.Fori(1, ND) as i:
                    hi(seg, i, *range(UF))

            def first():
                hi(up1, 0, 0, 1)
                for q in range(4):
                    act.wait_ge(x_loaded[q], 16)
                    blocks = slice(4 * q, 4 * q + 4)
                    act.activation(xT_hi[:, blocks], x_stage[:, blocks], ACT.Copy).then_inc(lhs_hi, 1)
                    hi(up1, 0, 2 + q)
                hi(up1, 0, 6, 7)

            up(up1, 0, t_up1, first)
            with act.Fori(1, NFF) as i:
                up(up1, i, t_up1, None)
            down(down1, t_up1)

            def conv_block(n):
                for t in range(TT):
                    act.wait_ge(tr_full, t_conv + 2 * n + t + 1)
                    act.activation(ch[:, BLK * n:BLK * (n + 1), PAD + t * P:PAD + (t + 1) * P],
                                   tb[:, t].rearrange("p (b n) -> p b n", b=BLK), ACT.Copy).then_inc(ch_ready, 1)

            def conv_gate(c, last):
                for t in range(TT):
                    tile_full(conv_in, 0, c, last, t)
                    act.activation(act_sb[:, t], acc[:, t], ACT.Sigmoid).then_inc(acc_out[0], 1)

            after_norm(conv_in, t_ln1)
            hi(conv_in, 0, 8, 9, 10, 11)
            conv_gate(0, UD - 1)
            hi(conv_in, 0, *range(12, 24))
            conv_block(0)
            hi(conv_in, 0, 24, 25, 26, 27)
            conv_gate(2, 3 * UD - 1)
            hi(conv_in, 0, 28, 29, 30, 31)
            hi(first_q, 0, *range(8))
            conv_block(1)

            with act.Fori(0, NG) as g:
                tg = TH * g + t_heads
                hi(heads, g, 0, 1, 2, 3)
                for t in range(TT):
                    if t == 0:
                        act.wait_ge(tile0_full, heads.chunk(g, 0))
                        act.wait_ge(tr_full, tg - TH + 4)
                    else:
                        act.wait_ge(unit_used, heads.unit(g, 0))
                    act.activation(act_sb[:, t], acc[:, t], ACT.Copy).then_inc(acc_out[0], 1)
                hi(heads, g, 4, 5, 6, 7)
                for t in range(TT):
                    act.wait_ge(tr_full, tg + (t + 1))
                    act.activation(qT[:, :, t * P:(t + 1) * P], tb[:, t].rearrange("p (b n) -> p b n", b=HG),
                                   ACT.Copy).then_inc(qk_ready, 1)
                hi(heads, g, 8, 9, 10, 11)
                for t in range(TT):
                    tile_full(heads, g, 0, UD - 1, t)
                    act.activation(act_sb[:, t], acc[:, 2 + t], ACT.Copy).then_inc(acc_out[1], 1)
                hi(heads, g, 12, 13, 14, 15)
                for t in range(TT):
                    act.wait_ge(tr_full, tg + (2 + t + 1))
                    act.activation(kT[:, :, t * P:(t + 1) * P], tb[:, 2 + t].rearrange("p (b n) -> p b n", b=HG),
                                   ACT.Copy).then_inc(qk_ready, 1)
                hi(heads, g, 16, 17, 18, 19)
                for t in range(TT):
                    tile_full(heads, g, 1, 2 * UD - 1, t)
                    act.activation(vt[:, t], acc[:, t], ACT.Copy).then_inc(acc_out[0], 1)
                hi(heads, g, 20, 21, 22, 23)
                act.wait_ge(smax_ready, 3 * g + 3)
                for h in range(HG):
                    for q, cols in enumerate((slice(0, P), slice(P, SC))):
                        n = HG * q + h
                        act.activation(pr[:, h, cols], pr[:, h, cols], ACT.Exp, bias=nmax[:, n:n + 1], scale=SCALE,
                                       accum_out=ssum[:, n:n + 1]).then_inc(exp_ready, 1)
                hi(heads, g, 24, 25, 26, 27)
                for t in range(TT):
                    tile_full(heads, g, 2, 3 * UD - 1, t)
                    act.activation(sig[:, bass.ds(g, 1), t], acc[:, 2 + t:3 + t], ACT.Sigmoid).then_inc(acc_out[1], 1)
                hi(heads, g, 28, 29, 30, 31)
                for h in range(HG):
                    act.wait_ge(tr_full, tg + (8 + h + 1))
                    act.activation(pT[:, h], tb[:, h, 0:SC], ACT.Copy).then_inc(pT_ready, 1)
                for b in range(2):
                    act.wait_ge(tr_full, tg + (12 + b + 1))
                    act.activation(oT_hi[:, bass.ds(4 * g + 2 * b, 2)],
                                   tb[:, b].rearrange("p (h n) -> p h n", h=2), ACT.Copy).then_inc(lhs_hi, 1)

            def conv_out_gate(i):
                for t in range(TT):
                    if t == 0:
                        act.wait_ge(tile0_full, gates.chunk(i - 1, 0))
                    else:
                        act.wait_ge(unit_used, gates.unit(i - 1, 0))
                    act.activation(sig[:, bass.ds(i + (ND - 1), 1), t], acc[:, t:t + 1],
                                   ACT.Sigmoid).then_inc(acc_out[0], 1)

            with act.Fori(1, ND) as i:
                hi(gates, i - 1, 0, 1, 2, 3)
                conv_out_gate(i)
                hi(gates, i - 1, 4, 5, 6, 7)

            hi(attn_out, 0, 0, 1, 2, 3)
            conv_out_gate(ND)
            hi(attn_out, 0, 4, 5, 6, 7)
            hi(attn_out, 1, 0, 1, 2, 3)
            for t in range(TT):
                act.wait_ge(ln_ready, 8 + t + 1)
                act.activation(ct[:, t], ct[:, t], ACT.Silu).then_inc(silu_ready, 1)
            hi(attn_out, 1, 4, 5, 6, 7)
            for t in range(TT):
                for half in range(2):
                    block_hi(cT_hi[:, BLK * half:BLK * (half + 1), t * P:(t + 1) * P], 2 * t + half,
                             t_convt + 2 * t + half + 1)
            with act.Fori(2, ND) as i:
                hi(attn_out, i, *range(UD))

            def merged_hi(c):
                for t in range(TT):
                    block_hi(oT_hi[:, BLK * c:BLK * (c + 1), t * P:(t + 1) * P], 2 * (c % 2) + t,
                             t_merge + 2 * c + t + 1)

            hi(conv_out, 0, *range(12))
            merged_hi(0)
            hi(conv_out, 0, 12, 13, 14, 15)
            merged_hi(1)

            hi(mix_out, 0, 0, 1, 2, 3)
            merged_hi(2)
            hi(mix_out, 0, 4, 5, 6, 7)
            merged_hi(3)
            with act.Fori(1, ND) as i:
                hi(mix_out, i, *range(UD))

            up(up2, 0, t_up2, lambda: after_norm(up2, t_ln2))
            with act.Fori(1, NFF) as i:
                up(up2, i, t_up2, None)
            down(down2, t_up2)

        @block.vector
        def _(dve):
            steps = [0]
            pieces_done = [0]

            def lo(seg, i, *units):
                for j in units:
                    dve.wait_ge(hi_ready, seg.unit(i, j) + 1)
                    s = seg.split(j)
                    dve.tensor_tensor(w_lo[:, s], raw[:, seg.raw(j)], f32(w_hi[:, s]),
                                      ALU.subtract).then_inc(lo_ready, 1)

            def tile_full(seg, i, c, last, t):
                if t == 0:
                    dve.wait_ge(tile0_full, seg.chunk(i, c) + 1)
                else:
                    dve.wait_ge(unit_used, seg.unit(i, last) + 1)

            def block_lo(dst, hi_part, bank, done):
                dve.wait_ge(lhs_hi, done)
                dve.tensor_tensor(dst, tb[:, bank].rearrange("p (b n) -> p b n", b=BLK), f32(hi_part),
                                  ALU.subtract).then_inc(lhs_lo, 1)

            def step(ins):
                ins.then_inc(ln_step, 1)
                steps[0] += 1
                return steps[0]

            def add_rows(t, cols, seg, i, uses):
                tile_full(seg, i, 0, seg.n - 1, t)
                dve.scalar_tensor_tensor(out=res[:, t, cols], in0=res[:, t, cols], scalar=ALPHA, in1=acc[:, t],
                                         op0=ALU.mult, op1=ALU.add).then_inc(acc_out[0], 1)

            def row_stats(t, c, cols, use):
                dve.wait_ge(acc_out[0], 2 * use + t + 1)
                return dve.bn_stats(stats[:, t, c], res[:, t, cols])

            def finish_stats(t, last, groups, n):
                dve.wait_ge(ln_step, step(last))
                done = step(dve.bn_aggr(mv[:, t], stats[:, t, 0:groups].rearrange("p a b -> p (a b)")))
                dve.wait_ge(ln_step, done)
                dve.tensor_scalar(var_eps[:, t], mv[:, t, 1:2], EPS, None, ALU.add).then_inc(var_ready, 1)
                dve.wait_ge(rstd_ready, n)

            def norm_pieces(t, pieces, gb):
                marks = []
                if pieces_done[0]:
                    dve.wait_ge(ln_ready, pieces_done[0])
                pieces_done[0] += len(pieces)
                for p in pieces:
                    cols = slice(p * COLS, (p + 1) * COLS)
                    marks.append(step(dve.scalar_tensor_tensor(
                        out=act_sb[:, p % 2], in0=res[:, t, cols], scalar=mv[:, t, 0:1], in1=gb[:, 0, cols],
                        op0=ALU.subtract, op1=ALU.mult)))
                for p, mark in zip(pieces, marks):
                    cols = slice(p * COLS, (p + 1) * COLS)
                    dve.wait_ge(ln_step, mark)
                    dve.scalar_tensor_tensor(out=res[:, t, cols], in0=act_sb[:, p % 2], scalar=rstd[:, t],
                                             in1=gb[:, 1, cols], op0=ALU.mult, op1=ALU.add).then_inc(ln_ready, 1)

            def norm_lo(t, pieces, done):
                for p in pieces:
                    blocks, rows = slice(BLK * p, BLK * (p + 1)), slice(t * P, (t + 1) * P)
                    block_lo(xT_lo[:, blocks, rows], xT_hi[:, blocks, rows], 2 * t + p % 2, done)
                    done += 1

            last_cols = slice((ND - 1) * COLS, D)

            def norm(seg, u0, n, b0, nxt):
                gb = ln_gb[n]
                use = u0 + ND - 1
                lo(nxt, 0, 0, 1, 2, 3)
                add_rows(0, last_cols, seg, ND - 1, use)
                dve.wait_ge(gb_loaded, 32 * (n + 1))
                finish_stats(0, row_stats(0, ND - 1, last_cols, use), ND, rs[0] + 1)
                norm_pieces(0, (0, 1), gb)
                norm_lo(0, (0, 1), b0 + 1)
                add_rows(1, last_cols, seg, ND - 1, use)
                finish_stats(1, row_stats(1, ND - 1, last_cols, use), ND, rs[0] + 2)
                dve.wait_ge(ln_step, steps[0])
                norm_pieces(1, (0, 1), gb)
                norm_lo(1, (0, 1), b0 + 3)
                norm_pieces(0, (2, 3), gb)
                norm_lo(0, (2, 3), b0 + 5)
                lo(nxt, 0, 4, 5, 6, 7)
                norm_pieces(1, (2, 3), gb)
                norm_lo(1, (2, 3), b0 + 7)
                rs[0] += 2

            rs = [0]

            def hidden(seg, i, last, use):
                for t in range(TT):
                    dve.wait_ge(acc_out[0], 2 * use + (t + 1))
                    tile_full(seg, i, 1, last, t)
                    dve.scalar_tensor_tensor(out=act_sb[:, t], in0=act_sb[:, t], scalar=0.5, in1=acc[:, 2 + t],
                                             op0=ALU.mult, op1=ALU.mult).then_inc(acc_out[1], 1)

            def hidden_lo(i, b0):
                for t in range(TT):
                    rows = slice(t * P, (t + 1) * P)
                    block_lo(hT_lo[:, bass.ds(BLK * i, BLK), rows], hT_hi[:, bass.ds(BLK * i, BLK), rows], t,
                              2 * i + (b0 + t + 1))

            def up(seg, u0, b0, start):
                start()
                lo(seg, 0, *range(8, 16))
                with dve.Fori(1, NFF) as i:
                    lo(seg, i, 0, 1, 2, 3)
                    hidden(seg, i - 1, 2 * UD - 1, i + (u0 - 1))
                    lo(seg, i, 4, 5, 6, 7)
                    hidden_lo(i - 1, b0)
                    lo(seg, i, *range(8, 16))

            def down(seg, before, u_up, u0, b0):
                lo(seg, 0, 0, 1, 2, 3)
                hidden(before, NFF - 1, 2 * UD - 1, u_up + NFF - 1)
                lo(seg, 0, 4, 5, 6, 7)
                hidden_lo(NFF - 1, b0)
                lo(seg, 0, *range(8, UF))
                with dve.Fori(1, ND) as i:
                    rows_before(seg, i, u0, lambda: lo(seg, i, 0, 1), lambda: lo(seg, i, 2, 3, 4))
                    lo(seg, i, *range(5, UF))

            def rows_before(seg, i, u0, ahead, between):
                cols = bass.ds(COLS * (i - 1), COLS)
                ahead()
                add_rows(0, cols, seg, i - 1, None)
                between()
                dve.wait_ge(acc_out[0], 2 * i + (2 * u0 - 1))
                dve.bn_stats(stats[:, 0, bass.ds(i - 1, 1)].rearrange("p a b -> p (a b)"), res[:, 0, cols])
                add_rows(1, cols, seg, i - 1, None)
                dve.wait_ge(acc_out[0], 2 * i + 2 * u0)
                dve.bn_stats(stats[:, 1, bass.ds(i - 1, 1)].rearrange("p a b -> p (a b)"), res[:, 1, cols])

            def first():
                lo(up1, 0, 0, 1)
                for q in range(4):
                    blocks = slice(4 * q, 4 * q + 4)
                    dve.wait_ge(lhs_hi, q + 1)
                    dve.tensor_tensor(xT_lo[:, blocks], x_stage[:, blocks], f32(xT_hi[:, blocks]),
                                      ALU.subtract).then_inc(lhs_lo, 1)
                    lo(up1, 0, 2 + q)
                lo(up1, 0, 6, 7)

            up(up1, 0, b_up1, first)
            dve.wait_ge(res_loaded, 16)
            down(down1, up1, 0, u0_down1, b_up1)
            norm(down1, u0_down1, 0, b_ln1, conv_in)

            def conv_value(c, last, use):
                for t in range(TT):
                    dve.wait_ge(acc_out[0], 2 * use + t + 1)
                    tile_full(conv_in, 0, c, last, t)
                    dve.tensor_tensor(act_sb[:, t], act_sb[:, t], acc[:, 2 + t], ALU.mult).then_inc(acc_out[1], 1)

            dve.memset(ch[:, :, 0:PAD], 0.0).then_inc(conv_step, 2)
            lo(conv_in, 0, *range(8, 20))
            conv_value(1, 2 * UD - 1, u0_conv)
            lo(conv_in, 0, *range(20, 32))
            lo(first_q, 0, 0, 1, 2, 3)
            conv_value(3, 4 * UD - 1, u0_conv + 1)
            lo(first_q, 0, 4, 5, 6, 7)
            dve.wait_ge(ch_ready, 4)
            dve.wait_ge(cw_loaded, 32)
            dve.wait_ge(alibi_loaded, 16)

            NT = 2 * TAPS
            with dve.Fori(0, NG) as g:
                tg = TH * g + t_heads

                def taps(first, count):
                    for n in range(first, min(first + count, NT)):
                        k, j = n % 2, n // 2
                        rows = ch[:, bass.ds(2 * g + k, 1), j:j + T].rearrange("p a n -> p (a n)")
                        w = cw[:, bass.ds(2 * TAPS * g + (k * TAPS + j), 1)]
                        dve.wait_ge(conv_step, NT * g + (n + 1))
                        if j == 0:
                            ins = dve.tensor_scalar(cacc[:, k], rows, w, cw[:, bass.ds(2 * g + (KC * TAPS + k), 1)],
                                                    ALU.mult, ALU.add)
                        else:
                            ins = dve.scalar_tensor_tensor(out=rows if j == TAPS - 1 else cacc[:, k], in0=rows,
                                                           scalar=w, in1=cacc[:, k], op0=ALU.mult, op1=ALU.add)
                        ins.then_inc(conv_step, 1)

                for j in range(20):
                    lo(heads, g, j)
                    taps(2 * j, 2)
                for h in range(HG):
                    dve.wait_ge(tr_full, tg + (4 + h + 1))
                    dve.scalar_tensor_tensor(out=pr[:, h], in0=alibi[:, 0:SC],
                                             scalar=alibi[:, bass.ds(HG * g + (SC + h), 1)],
                                             in1=tb[:, h, 0:SC], op0=ALU.mult, op1=ALU.add).then_inc(s_ready, 1)
                dve.wait_ge(s_ready, HG * g + HG)
                dve.tensor_reduce(smax[:, 0:HG], pr[:, :, 0:P], AX_X, ALU.max).then_inc(smax_ready, 1)
                dve.tensor_reduce(smax[:, HG:2 * HG], pr[:, :, P:SC], AX_X, ALU.max).then_inc(smax_ready, 1)
                dve.wait_ge(smax_ready, 3 * g + 2)
                dve.tensor_scalar(nmax[:], smax[:], -SCALE, None, ALU.mult).then_inc(smax_ready, 1)
                for j in range(20, 24):
                    lo(heads, g, j)
                    taps(2 * j, 2)
                lo(heads, g, 24)
                dve.wait_ge(exp_ready, 2 * HG * g + 2 * HG)
                dve.reciprocal(rsum[:], ssum[:]).then_inc(p_ready, 1)
                dve.wait_ge(p_ready, (2 * HG + 1) * g + 1)
                for h in range(HG):
                    for q, cols in enumerate((slice(0, P), slice(P, SC))):
                        n = HG * q + h
                        dve.tensor_scalar(pr[:, h, cols], pr[:, h, cols], rsum[:, n:n + 1], None,
                                          ALU.mult).then_inc(p_ready, 1)
                taps(48, 2)
                for j in range(25, 32):
                    lo(heads, g, j)
                    taps(2 * j, 2)
                for b in range(2):
                    two = bass.ds(4 * g + 2 * b, 2)
                    dve.wait_ge(lhs_hi, 2 * g + (b_heads + b + 1))
                    dve.tensor_tensor(oT_lo[:, two], tb[:, b].rearrange("p (h n) -> p h n", h=2), f32(oT_hi[:, two]),
                                      ALU.subtract).then_inc(lhs_lo, 1)

            with dve.Fori(0, ND - 1) as i:
                lo(gates, i, *range(UD))

            def attn_rows(i):
                for t in range(TT):
                    tile_full(attn_out, i - 1, 0, UD - 1, t)
                    g = sig[:, bass.ds(i - 1, 1), t]
                    dve.tensor_tensor(g, g, acc[:, 2 + t:3 + t], ALU.mult).then_inc(acc_out[1], 1)

            lo(attn_out, 0, 0, 1, 2, 3, 4, 5)
            dve.wait_ge(cgb_loaded, 32)
            for t in range(TT):
                lo(attn_out, 0, 6 + t)
                for half in range(2):
                    dve.wait_ge(tr_full, t_convo + 2 * t + half + 1)
                    last = dve.bn_stats(stats[:, t, half], tb[:, 2 * t + half])
                    if half == 0:
                        step(last)
                finish_stats(t, last, 2, rs[0] + 1 + t)
                marks = []
                for half in range(2):
                    cols = slice(half * COLS, (half + 1) * COLS)
                    marks.append(step(dve.scalar_tensor_tensor(
                        out=ct[:, t, cols], in0=tb[:, 2 * t + half], scalar=mv[:, t, 0:1], in1=cgb[:, 0, cols],
                        op0=ALU.subtract, op1=ALU.mult)))
                dve.wait_ge(ln_step, marks[-1])
                dve.scalar_tensor_tensor(out=ct[:, t], in0=ct[:, t], scalar=rstd[:, t], in1=cgb[:, 1],
                                         op0=ALU.mult, op1=ALU.add).then_inc(ln_ready, 1)
            rs[0] += 2
            pieces_done[0] += 2
            lo(attn_out, 1, 0, 1, 2, 3)
            attn_rows(1)
            lo(attn_out, 1, 4, 5, 6, 7)
            for t in range(TT):
                for half in range(2):
                    blocks, rows = slice(BLK * half, BLK * (half + 1)), slice(t * P, (t + 1) * P)
                    block_lo(cT_lo[:, blocks, rows], cT_hi[:, blocks, rows], 2 * t + half,
                              b_convt + 2 * t + half + 1)
            with dve.Fori(2, ND) as i:
                lo(attn_out, i, 0, 1, 2, 3)
                attn_rows(i)
                lo(attn_out, i, 4, 5, 6, 7)

            def merge(c):
                for t in range(TT):
                    tile_full(conv_out, 0, c, UC * (c + 1) - 1, t)
                    dve.tensor_tensor(sig[:, ND + c, t], sig[:, ND + c, t], acc[:, t], ALU.mult).then_inc(acc_out[0], 1)
                for t in range(TT):
                    dve.wait_ge(acc_out[0], 2 * (u0_convo + c) + t + 1)
                    dve.tensor_tensor(sig[:, c, t], sig[:, c, t], sig[:, ND + c, t], ALU.add).then_inc(merged, 1)

            def merged_lo(c):
                for t in range(TT):
                    blocks, rows = slice(BLK * c, BLK * (c + 1)), slice(t * P, (t + 1) * P)
                    block_lo(oT_lo[:, blocks, rows], oT_hi[:, blocks, rows], 2 * (c % 2) + t,
                              b_merge + 2 * c + t + 1)

            lo(conv_out, 0, 0, 1, 2, 3)
            attn_rows(ND)
            lo(conv_out, 0, 4, 5, 6, 7)
            merge(0)
            lo(conv_out, 0, 8, 9, 10, 11)
            merged_lo(0)
            merge(1)
            lo(conv_out, 0, 12, 13, 14, 15)
            merged_lo(1)
            merge(2)
            lo(mix_out, 0, 0, 1, 2, 3)
            merged_lo(2)
            merge(3)
            lo(mix_out, 0, 4, 5, 6, 7)
            merged_lo(3)
            with dve.Fori(1, ND) as i:
                rows_before(mix_out, i, u0_mix, lambda: lo(mix_out, i, 0, 1, 2, 3), lambda: None)
                lo(mix_out, i, 4, 5, 6, 7)

            up(up2, u0_up2, b_up2, lambda: norm(mix_out, u0_mix, 1, b_ln2, up2))
            down(down2, up2, u0_up2, u0_down2, b_up2)

            use = u0_down2 + ND - 1
            for t in range(TT):
                add_rows(t, last_cols, down2, ND - 1, use)
                if t == 0:
                    dve.wait_ge(gb_loaded, 96)
                finish_stats(t, row_stats(t, ND - 1, last_cols, use), ND, rs[0] + 1 + t)
                norm_pieces(t, (0, 1), ln_gb[2])
                norm_pieces(t, (2, 3), ln_gb[2])

        @block.gpsimd
        def _(pool):
            nc.gpsimd.memset(minus_half[:], -0.5).then_inc(half_ready, 1)
            pool.wait_ge(half_ready, 1)
            for n in range(4 * TT):
                pool.wait_ge(var_ready, n + 1)
                nc.gpsimd.tensor_tensor(rstd[:, n % TT], var_eps[:, n % TT], minus_half[:],
                                        ALU.pow).then_inc(rstd_ready, 1)

        @block.tensor
        def _(pe):
            def half_chunk(seg, i, units, pair, t, x_hi, x_lo, k0, first, last):
                rows = slice(t * P, (t + 1) * P)
                out_ap = acc[:, 2 * pair + t]
                for n, j in enumerate(units):
                    if t == 0:
                        pe.wait_ge(lo_ready, seg.unit(i, j) + 1)
                    s = seg.split(j)
                    for b in range(UK):
                        k = k0 + UK * n + b
                        cols = slice(b * COLS, (b + 1) * COLS)
                        begin = first and n == 0 and b == 0
                        end = last and n == len(units) - 1 and b == UK - 1
                        pe.matmul(out_ap, x_hi[:, k, rows], w_hi[:, s, cols], start=begin, stop=False)
                        pe.matmul(out_ap, x_lo[:, k, rows], w_hi[:, s, cols], start=False, stop=False)
                        mm = pe.matmul(out_ap, x_hi[:, k, rows], w_lo[:, s, cols], start=False, stop=end)
                    if t == 1:
                        mm.then_inc(unit_used, 1)
                if t == 0 and last:
                    mm.then_inc(tile0_full, 1)

            def chunk(seg, i, j0, n, pair, x, use, tile_uses=None, after=None, ready=None):
                groups, at_unit = [], j0
                size = (n - 1) % GROUP + 1
                while at_unit < j0 + n:
                    groups.append(range(at_unit, at_unit + size))
                    at_unit += size
                    size = GROUP
                for q, units in enumerate(groups):
                    for t in range(TT):
                        if q == 0:
                            v = use if isinstance(use, int) and use == 0 else 2 * use + (t - 1)
                            if not (isinstance(v, int) and v <= 0):
                                pe.wait_ge(acc_out[pair], v)
                        if ready and (q, t) in ready:
                            ready[(q, t)]()
                        half_chunk(seg, i, units, pair, t, x[0], x[1], UK * (units[0] - j0), q == 0,
                                   q == len(groups) - 1)
                        if after and (q, t) in after:
                            after[(q, t)]()

            def turn(bank, blocks):
                for n, b in enumerate(blocks):
                    mm = pe.transpose(tb[:, bank, n * P:(n + 1) * P], b, ident[:])
                mm.then_inc(tr_full, 1)

            def turn_act(bank, t):
                turn(bank, [act_sb[:, t, n * P:(n + 1) * P] for n in range(BLK)])

            xT = (xT_hi, xT_lo)
            hT = (hT_hi, hT_lo)
            oT = (oT_hi, oT_lo)
            cT = (cT_hi, cT_lo)

            def wait_lhs(n):
                return lambda: pe.wait_ge(lhs_lo, n)

            def turn_hidden(i, u1, b0):
                for t in range(TT):
                    pe.wait_ge(acc_out[1], 2 * i + (2 * u1 + t + 1))
                    pe.wait_ge(lhs_lo, 2 * i + (b0 + t - 1))
                    turn_act(t, t)

            def up(seg, u0, u1, b0, start, ready):
                chunk(seg, 0, 0, UD, 0, xT, u0, after=start, ready=ready)
                chunk(seg, 0, UD, UD, 1, xT, u1)
                with pe.Fori(1, NFF) as i:
                    chunk(seg, i, 0, UD, 0, xT, i + u0, after={(0, 0): lambda: turn_hidden(i - 1, u1, b0)})
                    chunk(seg, i, UD, UD, 1, xT, i + u1)

            def down(seg, u0, u1, b0):
                chunk(seg, 0, 0, UF, 0, hT, u0,
                      ready={(0, 0): wait_lhs(b0 + 2 * (NFF - 1)), (5, 0): wait_lhs(b0 + 2 * NFF)},
                      after={(0, 1): lambda: turn_hidden(NFF - 1, u1, b0)})
                with pe.Fori(1, ND) as i:
                    chunk(seg, i, 0, UF, 0, hT, i + u0)

            def turn_rows(t, pieces, r0, b0):
                for n, p in enumerate(pieces):
                    pe.wait_ge(ln_ready, r0 + n + 1)
                    pe.wait_ge(lhs_lo, b0)
                    turn(2 * t + p % 2, [res[:, t, p * COLS + k * P:p * COLS + (k + 1) * P] for k in range(BLK)])

            def norm_turns(r0, b0):
                after = {
                    (0, 0): lambda: turn_rows(1, (0, 1), r0 + 2, b0),
                    (0, 1): lambda: (turn_rows(0, (2, 3), r0 + 4, b0 + 2), turn_rows(1, (2, 3), r0 + 6, b0 + 4)),
                }
                ready = {(0, 0): wait_lhs(b0 + 2), (0, 1): wait_lhs(b0 + 4),
                         (1, 0): wait_lhs(b0 + 6), (1, 1): wait_lhs(b0 + 8)}
                return after, ready

            pe.wait_ge(ident_loaded, 16)
            up(up1, 0, 0, b_up1, None, {(0, 0): wait_lhs(2), (1, 0): wait_lhs(4)})
            down(down1, u0_down1, 0, b_up1)

            def turn_conv(n):
                for t in range(TT):
                    pe.wait_ge(acc_out[1], 2 * (NFF + n) + t + 1)
                    if n == 1:
                        pe.wait_ge(ch_ready, t + 1)
                    turn_act(t, t)

            turn_rows(0, (0, 1), 0, b_ln1)
            after, ready = norm_turns(0, b_ln1)
            chunk(conv_in, 0, 0, UD, 0, xT, u0_conv, after=after, ready=ready)
            chunk(conv_in, 0, UD, UD, 1, xT, NFF)
            chunk(conv_in, 0, 2 * UD, UD, 0, xT, u0_conv + 1, after={(0, 0): lambda: turn_conv(0)})
            chunk(conv_in, 0, 3 * UD, UD, 1, xT, NFF + 1)
            chunk(first_q, 0, 0, UD, 0, xT, u0_q, after={(0, 0): lambda: turn_conv(1)})
            pe.wait_ge(ch_ready, 4)

            with pe.Fori(0, NG) as g:
                def turn_q():
                    for t in range(TT):
                        pe.wait_ge(acc_out[0], 2 * (2 * g) + (2 * u0_heads + t - 1))
                        pe.wait_ge(lhs_lo, 2 * g + b_heads)
                        turn_act(t, t)

                def turn_k():
                    for t in range(TT):
                        pe.wait_ge(acc_out[1], 2 * (2 * g) + (2 * u1_heads + t + 1))
                        turn_act(2 + t, t)

                def scores():
                    pe.wait_ge(qk_ready, 4 * g + 4)
                    for h in range(HG):
                        pe.matmul(tb[:, h, 0:P], qT[:, h, 0:P], kT[:, h, 0:P], start=True, stop=True)
                        pe.matmul(tb[:, h, P:SC], qT[:, h, P:T], kT[:, h, :], start=True,
                                  stop=True).then_inc(tr_full, 1)

                def turn_p():
                    pe.wait_ge(p_ready, (2 * HG + 1) * g + (2 * HG + 1))
                    for h in range(HG):
                        turn(h, [pr[:, h, n * P:(n + 1) * P] for n in range(3)])

                def outputs():
                    pe.wait_ge(pT_ready, HG * g + HG)
                    for h in range(HG):
                        o = tb[:, h // 2, (h % 2) * T:(h % 2 + 1) * T]
                        cols = slice(h * DH, (h + 1) * DH)
                        pe.matmul(o, vt[:, 0, cols], pT[:, h, 0:T], start=True, stop=False)
                        mm = pe.matmul(o[:, P:T], vt[:, 1, cols], pT[:, h, T:SC], start=False, stop=True)
                        if h % 2 == 1:
                            mm.then_inc(tr_full, 1)

                chunk(heads, g, 0, UD, 1, xT, 2 * g + u1_heads, after={(0, 0): turn_q})
                chunk(heads, g, UD, UD, 0, xT, 2 * g + u0_heads, after={(0, 0): turn_k, (1, 0): scores})
                chunk(heads, g, 2 * UD, UD, 1, xT, 2 * g + (u1_heads + 1))
                chunk(heads, g, 3 * UD, UD, 0, xT, 2 * g + (u0_heads + 1), after={(0, 0): turn_p, (0, 1): outputs})

            with pe.Fori(0, ND - 1) as i:
                chunk(gates, i, 0, UD, 0, xT, i + u0_gates)

            def turn_conv_out():
                pe.wait_ge(conv_step, 2 * TAPS * NG + 2)
                for t in range(TT):
                    for half in range(2):
                        turn(2 * t + half, [ch[:, BLK * half + n, PAD + t * P:PAD + (t + 1) * P] for n in range(BLK)])

            def turn_conv_rows():
                for t in range(TT):
                    pe.wait_ge(silu_ready, t + 1)
                    for half in range(2):
                        turn(2 * t + half, [ct[:, t, half * COLS + n * P:half * COLS + (n + 1) * P] for n in range(BLK)])

            chunk(attn_out, 0, 0, UD, 1, oT, u1_attn, ready={(0, 0): wait_lhs(b_convt)}, after={(0, 0): turn_conv_out})
            chunk(attn_out, 1, 0, UD, 1, oT, u1_attn + 1, after={(1, 0): turn_conv_rows})
            with pe.Fori(2, ND) as i:
                chunk(attn_out, i, 0, UD, 1, oT, i + u1_attn)

            def turn_merged(c):
                for t in range(TT):
                    pe.wait_ge(merged, 2 * c + t + 1)
                    if c >= 2:
                        pe.wait_ge(lhs_lo, b_merge + 2 * (c - 2) + t + 1)
                    turn(2 * (c % 2) + t, [sig[:, c, t, n * P:(n + 1) * P] for n in range(BLK)])

            for c in range(ND):
                chunk(conv_out, 0, c * UC, UC, 0, cT, u0_convo + c, ready={(0, 0): wait_lhs(b_merge)} if c == 0 else None,
                      after={(0, 0): lambda: turn_merged(c - 1)} if c else None)

            chunk(mix_out, 0, 0, UD, 0, oT, u0_mix, ready={(0, 0): wait_lhs(b_merge + 4), (1, 0): wait_lhs(b_ln2)},
                  after={(0, 0): lambda: turn_merged(ND - 1)})
            with pe.Fori(1, ND) as i:
                chunk(mix_out, i, 0, UD, 0, oT, i + u0_mix)

            turn_rows(0, (0, 1), 10, b_ln2)
            after, ready = norm_turns(10, b_ln2)
            up(up2, u0_up2, u1_up2, b_up2, after, ready)
            down(down2, u0_down2, u1_up2, b_up2)


def units_of(w, col0):
    c = w[:, col0:col0 + COLS]
    return c.reshape(-1, UK, P, COLS).transpose(0, 2, 1, 3).reshape(-1, P, UNIT)


def weight_stream(i):
    q0, k0, v0, u0 = 0, D, 2 * D, 3 * D
    ga0, gc0 = 3 * D + 2 * CC, 4 * D + 2 * CC
    w_in = i["w_in"][0]
    parts = []

    def ffn(wg, wu, wd):
        for c in range(NFF):
            parts.extend([units_of(wg, c * COLS), units_of(wu, c * COLS)])
        parts.extend(units_of(wd, c * COLS) for c in range(ND))

    ffn(i["ffn1_wg"][0], i["ffn1_wu"][0], i["ffn1_wd"][0])
    for c in range(2):
        parts.extend([units_of(w_in, u0 + CC + c * COLS), units_of(w_in, u0 + c * COLS)])
    parts.append(units_of(w_in, q0))
    for g in range(NG):
        parts.extend([units_of(w_in, k0 + g * COLS), units_of(w_in, v0 + g * COLS), units_of(w_in, ga0 + g * COLS)])
        parts.append(units_of(w_in, q0 + (g + 1) * COLS if g + 1 < NG else gc0))
    parts.extend(units_of(w_in, gc0 + c * COLS) for c in range(1, ND))
    parts.extend(units_of(i["w_attn_out"][0], c * COLS) for c in range(ND))
    parts.extend(units_of(i["w_conv_out"][0], c * COLS) for c in range(ND))
    parts.extend(units_of(i["w_out"][0], c * COLS) for c in range(ND))
    ffn(i["ffn2_wg"][0], i["ffn2_wu"][0], i["ffn2_wd"][0])
    return np.concatenate(parts, axis=0)


def shape_constants():
    c = np.zeros((P, P + SC + H), np.float32)
    c[:, 0:P] = np.eye(P, dtype=np.float32)
    q = np.arange(P)[:, None]
    k = np.arange(P)[None, :]
    causal = np.where(k <= q, k - q, -1e37)
    c[:, P:P + SC] = np.concatenate([causal, k - (q + P), causal], axis=1)
    c[:, P + SC:] = [2.0 ** (-8.0 * (h + 1) / H) / SCALE for h in range(H)]
    return c


def kernel(**inputs):
    import concourse.bacc as _bacc
    from concourse.bass_utils import run_bass_kernel_spmd as _run

    i = {k: np.ascontiguousarray(v) for k, v in inputs.items()}
    x = i["x"][0]
    arrays = {
        "stream": weight_stream(i),
        "xT": np.ascontiguousarray(x.T.reshape(KD, P, T).transpose(1, 0, 2)),
        "x_rows": np.ascontiguousarray(x.reshape(TT, P, D).transpose(1, 0, 2)),
        "ln": np.concatenate([i[n] for n in ("ln1_g", "ln1_b", "ln2_g", "ln2_b", "ln3_g", "ln3_b")]),
        "conv_ln": np.concatenate([i["conv_ln_g"], i["conv_ln_b"]]),
        "conv_w": np.ascontiguousarray(i["conv_dw"][0, :, 0].reshape(TAPS, KC, P).transpose(2, 1, 0).reshape(P, -1)),
        "conv_b": np.ascontiguousarray(i["conv_db"][0].reshape(KC, P).T),
        "consts": shape_constants(),
    }
    nc = _bacc.Bacc("TRN2", target_bir_lowering=False, num_devices=1, dynamic_dma_scratch_size=1024)
    args = [nc.dram_tensor(f"in_{n}", a.shape, mybir.dt.from_np(a.dtype), kind="ExternalInput").ap()
            for n, a in arrays.items()]
    out = nc.dram_tensor("out_0", (T, D), F32, kind="ExternalOutput").ap()
    build(nc, *args, out)
    r = _run(nc, [{f"in_{n}": a for n, a in arrays.items()}], core_ids=[0])
    return r.results[0]["out_0"].reshape(1, T, D)
```

```python
from contextlib import ExitStack

import numpy as np

import concourse.bass as bass
from concourse import mybir

F32 = mybir.dt.float32
F32R = mybir.dt.float32r
ACT = mybir.ActivationFunctionType
ALU = mybir.AluOpType
AX_X = mybir.AxisListType.X

P = 128
D = 2048
T = 256
TT = T // P
FF = 5632
H = 16
DH = 128
CC = 1024
TAPS = 31
PAD = TAPS - 1
EPS = 1e-5
ALPHA = 2.0 ** 0.25
SCALE = DH ** -0.5
COLS = 512
UK = 2
UNIT = UK * COLS
RAW = 4
SPLIT = 8
GROUP = 4

KD = D // P
UD = KD // UK
KF = FF // P
UF = KF // UK
KC = CC // P
UC = KC // UK
NFF = FF // COLS
ND = D // COLS
BLK = COLS // P
HG = 4
NG = H // HG
NORM_ORDER = ((0, 0), (0, 1), (1, 0), (1, 1), (0, 2), (0, 3), (1, 2), (1, 3))
START = ((slice(0, 2), (0,)), (slice(2, 4), (1,)), (slice(4, 8), (2, 3)), (slice(8, 12), (4, 5)),
         (slice(12, 16), (6, 7)))
SC = 3 * P


class Segment:

    def __init__(self, before, n, chunks, iters):
        self.n, self.chunks, self.iters = n, chunks, iters
        if before is None:
            self.unit0, self.chunk0, self.raw0, self.split0, self.loads0 = 0, 0, 0, 0, [0] * RAW
        else:
            b = before
            self.unit0 = b.unit0 + b.n * b.iters
            self.chunk0 = b.chunk0 + b.chunks * b.iters
            self.raw0, self.split0 = (b.raw0 + b.n) % RAW, (b.split0 + b.n) % SPLIT
            self.loads0 = [x + y * b.iters for x, y in zip(b.loads0, b.loads_per_iteration())]

    def loads_per_iteration(self):
        return [sum(self.raw(j) == s for j in range(self.n)) for s in range(RAW)]

    def raw(self, j):
        return (self.raw0 + j) % RAW

    def split(self, j):
        return (self.split0 + j) % SPLIT

    def unit(self, i, j):
        return self.n * i + (self.unit0 + j)

    def loaded(self, i, j):
        s = self.raw(j)
        earlier = sum(self.raw(k) == s for k in range(j))
        return 16 * self.loads_per_iteration()[s] * i + 16 * (self.loads0[s] + earlier + 1)

    def before(self, i, j, slots):
        back = slots
        if self.n % slots and not (isinstance(i, int) and i == 0):
            back = self.n % slots if j < self.n % slots else self.n % slots + slots
            if j >= slots:
                back = slots
        v = self.unit(i, j) + 1 - back
        return None if isinstance(v, int) and v <= 0 else v

    def chunk(self, i, c):
        return self.chunks * i + (self.chunk0 + c)


def segments():
    up1 = Segment(None, 2 * UD, 2, NFF)
    down1 = Segment(up1, UF, 1, ND)
    conv_in = Segment(down1, 4 * UD, 4, 1)
    first_q = Segment(conv_in, UD, 1, 1)
    heads = Segment(first_q, 4 * UD, 4, NG)
    gates = Segment(heads, UD, 1, ND - 1)
    attn_out = Segment(gates, UD, 1, ND)
    conv_out = Segment(attn_out, ND * UC, ND, 1)
    mix_out = Segment(conv_out, UD, 1, ND)
    up2 = Segment(mix_out, 2 * UD, 2, NFF)
    down2 = Segment(up2, UF, 1, ND)
    return up1, down1, conv_in, first_q, heads, gates, attn_out, conv_out, mix_out, up2, down2


def build(nc, stream, xT, x, ln, conv_ln, conv_w, conv_b, consts, out):
    up1, down1, conv_in, first_q, heads, gates, attn_out, conv_out, mix_out, up2, down2 = segments()

    ctx = ExitStack()
    with ctx:
        base = -(-nc.sbuf_base // 64) * 64
        top = [base]

        def place(name, shape, dt=F32, at=None):
            size = 4 * int(np.prod(shape[1:]))
            if at is None:
                at = top[0]
                top[0] += -(-size // 32) * 32
            return nc.alloc_sbuf_tensor_at(name, shape, dt, offset=at)

        raw = place("raw", [P, RAW, UNIT])
        w_hi = place("w_hi", [P, SPLIT, UNIT], F32R)
        w_lo = place("w_lo", [P, SPLIT, UNIT], F32R)
        res = place("res", [P, TT, D])
        x_at = top[0]
        xT_hi = place("xT_hi", [P, KD, T], F32R)
        xT_lo = place("xT_lo", [P, KD, T], F32R)
        hid_at = top[0]
        hT_hi = place("hT_hi", [P, KF, T], F32R)
        hT_lo = place("hT_lo", [P, KF, T], F32R)
        hid_end = top[0]
        act_sb = place("act_sb", [P, TT, COLS])
        ident = place("ident", [P, P])
        stats = place("stats", [P, TT, ND, 6])
        mv = place("mv", [P, TT, 2])
        var_eps = place("var_eps", [P, TT, 1])
        rstd = place("rstd", [P, TT, 1])
        minus_half = place("minus_half", [P, 1])
        smax = place("smax", [P, 2 * HG])
        nmax = place("nmax", [P, 2 * HG])
        ssum = place("ssum", [P, 2 * HG])
        rsum = place("rsum", [P, 2 * HG])
        assert top[0] <= nc.sbuf_usable_end, (top[0], nc.sbuf_usable_end)
        x_stage = place("x_stage", [P, KD, T], at=hid_at)
        ln_gb = {0: place("ln1_gb", [P, 2, D], at=hid_at)}
        ln_gb[2] = ln_gb[0]
        at = [hid_at]

        def mix(name, shape, dt=F32):
            t = place(name, shape, dt, at=at[0])
            at[0] += 4 * int(np.prod(shape[1:]))
            return t

        sig = mix("sig", [P, 2 * ND, TT, COLS])
        oT_hi = mix("oT_hi", [P, H, T], F32R)
        oT_lo = mix("oT_lo", [P, H, T], F32R)
        qT = mix("qT", [P, HG, T])
        kT = mix("kT", [P, HG, T])
        vt = mix("vt", [P, TT, COLS])
        ch = mix("ch", [P, KC, PAD + T])
        alibi = mix("alibi", [P, SC + H])
        cw = mix("cw", [P, KC * TAPS + KC])
        assert at[0] <= hid_end
        gc_at = hid_at + 4 * ND * TT * COLS
        pr = place("pr", [P, HG, SC], at=gc_at)
        pT = place("pT", [P, HG, SC], at=gc_at + 4 * HG * SC)
        cacc = place("cacc", [P, 2, T], at=gc_at + 8 * HG * SC)
        ln_gb[1] = place("ln2_gb", [P, 2, D], at=gc_at)
        cT_hi = place("cT_hi", [P, KC, T], F32R, at=x_at)
        cT_lo = place("cT_lo", [P, KC, T], F32R, at=x_at + 4 * KC * T)
        ct = place("ct", [P, TT, CC], at=x_at + 8 * KC * T)
        cgb = place("cgb", [P, 2, CC], at=x_at + 8 * KC * T + 4 * TT * CC)

        acc = ctx.enter_context(nc.psum_tensor("acc", [P, 4, COLS], F32))
        tb = ctx.enter_context(nc.psum_tensor("tb", [P, 4, COLS], F32))

        def sem(name):
            return ctx.enter_context(nc.semaphore(name))

        raw_loaded = [sem(f"raw_loaded{s}") for s in range(RAW)]
        hi_ready = sem("hi_ready")
        lo_ready = sem("lo_ready")
        unit_used = sem("unit_used")
        tile0_full = sem("tile0_full")
        acc_out = [sem("acc_out0"), sem("acc_out1")]
        tr_full = sem("tr_full")
        lhs_hi = sem("lhs_hi")
        lhs_lo = sem("lhs_lo")
        x_loaded = [sem(f"x_loaded{q}") for q in range(len(START))]
        res_loaded = sem("res_loaded")
        ident_loaded = sem("ident_loaded")
        gb_loaded = sem("gb_loaded")
        cgb_loaded = sem("cgb_loaded")
        alibi_loaded = sem("alibi_loaded")
        cw_loaded = sem("cw_loaded")
        half_ready = sem("half_ready")
        ln_step = sem("ln_step")
        var_ready = sem("var_ready")
        rstd_ready = sem("rstd_ready")
        ln_ready = sem("ln_ready")
        ch_ready = sem("ch_ready")
        conv_step = sem("conv_step")
        qk_ready = sem("qk_ready")
        s_ready = sem("s_ready")
        smax_ready = sem("smax_ready")
        exp_ready = sem("exp_ready")
        p_ready = sem("p_ready")
        pT_ready = sem("pT_ready")
        silu_ready = sem("silu_ready")
        gated = sem("gated")
        merged = sem("merged")
        stored = sem("stored")

        u0_down1 = NFF
        u0_conv = u0_down1 + ND
        u0_q = u0_conv + 2
        u0_heads = u0_q + 1
        u1_heads = NFF + 2
        u0_gates = u0_heads + 2 * NG
        u1_attn = u1_heads + 2 * NG
        u0_convo = u0_gates + ND - 1
        u0_mix = u0_convo + ND
        u0_up2 = u0_mix + ND
        u1_up2 = u1_attn + ND
        u0_down2 = u0_up2 + NFF
        b_up1 = len(START)
        b_ln1 = b_up1 + 2 * NFF
        b_heads = b_ln1 + 8
        b_convt = b_heads + 2 * NG
        b_merge = b_convt + 4
        b_ln2 = b_merge + 2 * ND
        b_up2 = b_ln2 + 8
        t_up1 = 0
        t_ln1 = 2 * NFF
        t_conv = t_ln1 + 8
        t_heads = t_conv + 4
        TH = 2 + 2 + HG + HG + 2
        t_convo = t_heads + TH * NG
        t_convt = t_convo + 4
        t_merge = t_convt + 4
        t_ln2 = t_merge + 2 * ND
        t_up2 = t_ln2 + 8

        def f32(ap):
            return ap.bitcast(F32)

        block = ctx.enter_context(nc.Block())

        @block.sync
        def _(sp):
            def load(seg, i, j):
                v = seg.before(i, j, RAW)
                if v is not None:
                    sp.wait_ge(lo_ready, v)
                src = stream[bass.ds(seg.unit(i, j), 1)].rearrange("a p n -> p (a n)")
                sp.dma_start(raw[:, seg.raw(j)], src).then_inc(raw_loaded[seg.raw(j)], 16)

            def loads(seg, first=0):
                with sp.Fori(first, seg.iters) as i:
                    for j in range(seg.n):
                        load(seg, i, j)

            def load_once(seg):
                for j in range(seg.n):
                    load(seg, 0, j)

            def load_gb(n, dst):
                for k in range(2):
                    sp.dma_start(dst[:, k], ln[2 * n + k:2 * n + k + 1].to_broadcast([P, D])).then_inc(gb_loaded, 16)

            for q, (blocks, units) in enumerate(START):
                sp.dma_start(x_stage[:, blocks], xT[:, blocks]).then_inc(x_loaded[q], 16)
                for j in units:
                    load(up1, 0, j)
            sp.dma_start(ident[:], consts[:, 0:P]).then_inc(ident_loaded, 16)
            load(up1, 0, UD)
            sp.dma_start(res[:], x).then_inc(res_loaded, 16)
            for j in range(UD + 1, up1.n):
                load(up1, 0, j)
            loads(up1, 1)
            load_once(down1)
            loads(down1, 1)
            sp.wait_ge(unit_used, down1.unit(ND - 1, UD))
            load_gb(0, ln_gb[0])
            load_once(conv_in)
            load_once(first_q)
            sp.dma_start(alibi[:], consts[:, P:P + SC + H]).then_inc(alibi_loaded, 16)
            sp.dma_start(cw[:, 0:KC * TAPS], conv_w).then_inc(cw_loaded, 16)
            sp.dma_start(cw[:, KC * TAPS:], conv_b).then_inc(cw_loaded, 16)
            loads(heads)
            loads(gates)
            for j in range(attn_out.n):
                load(attn_out, 0, j)
            sp.wait_ge(unit_used, attn_out.unit(0, 0))
            for k in range(2):
                sp.dma_start(cgb[:, k], conv_ln[k:k + 1].to_broadcast([P, CC])).then_inc(cgb_loaded, 16)
            loads(attn_out, 1)
            load_once(conv_out)
            load_once(mix_out)
            sp.wait_ge(merged, 2 * ND)
            load_gb(1, ln_gb[1])
            loads(mix_out, 1)
            loads(up2)
            load_once(down2)
            loads(down2, 1)
            sp.wait_ge(unit_used, down2.unit(ND - 1, UD))
            load_gb(2, ln_gb[2])
            for n, (t, p) in enumerate((t, p) for t in range(TT) for p in range(ND)):
                sp.wait_ge(ln_ready, 18 + n + 1)
                cols = slice(p * COLS, (p + 1) * COLS)
                sp.dma_start(out[t * P:(t + 1) * P, cols], res[:, t, cols]).then_inc(stored, 16)
            sp.wait_ge(stored, 16 * TT * ND)

        @block.scalar
        def _(act):
            def hi(seg, i, *units):
                for j in units:
                    v = seg.before(i, j, SPLIT)
                    if v is not None:
                        act.wait_ge(unit_used, v)
                    act.wait_ge(raw_loaded[seg.raw(j)], seg.loaded(i, j))
                    act.activation(w_hi[:, seg.split(j)], raw[:, seg.raw(j)], ACT.Copy).then_inc(hi_ready, 1)

            def tile_full(seg, i, c, last, t):
                if t == 0:
                    act.wait_ge(tile0_full, seg.chunk(i, c) + 1)
                else:
                    act.wait_ge(unit_used, seg.unit(i, last) + 1)

            def block_hi(dst, bank, filled):
                act.wait_ge(tr_full, filled)
                act.activation(dst, tb[:, bank].rearrange("p (b n) -> p b n", b=BLK), ACT.Copy).then_inc(lhs_hi, 1)

            def gate(seg, i, func):
                for t in range(TT):
                    tile_full(seg, i, 0, UD - 1, t)
                    act.activation(act_sb[:, t], acc[:, t], func).then_inc(acc_out[0], 1)

            def after_norm(seg, t0):
                def piece_hi(n):
                    t, p = NORM_ORDER[n]
                    block_hi(xT_hi[:, BLK * p:BLK * (p + 1), t * P:(t + 1) * P], 2 * t + p % 2, t0 + n + 1)

                hi(seg, 0, 0, 1, 2, 3)
                piece_hi(0)
                hi(seg, 0, 4)
                piece_hi(1)
                hi(seg, 0, 5)
                piece_hi(2)
                piece_hi(3)
                hi(seg, 0, 6)
                piece_hi(4)
                piece_hi(5)
                hi(seg, 0, 7)
                piece_hi(6)
                piece_hi(7)

            def hidden_hi(i, t0):
                for t in range(TT):
                    block_hi(hT_hi[:, bass.ds(BLK * i, BLK), t * P:(t + 1) * P], t, 2 * i + (t0 + t + 1))

            def up(seg, i, t0, start):
                if start is None:
                    hi(seg, i, 0, 1, 2, 3, 4, 5, 6, 7)
                    hidden_hi(i - 1, t0)
                else:
                    start()
                hi(seg, i, 8, 9, 10, 11)
                gate(seg, i, ACT.Silu)
                hi(seg, i, 12, 13, 14, 15)

            def down(seg, t0):
                hi(seg, 0, *range(8))
                hidden_hi(NFF - 1, t0)
                hi(seg, 0, *range(8, UF))
                with act.Fori(1, ND) as i:
                    hi(seg, i, *range(UF))

            def first():
                for q, (blocks, units) in enumerate(START):
                    act.wait_ge(x_loaded[q], 16)
                    act.activation(xT_hi[:, blocks], x_stage[:, blocks], ACT.Copy).then_inc(lhs_hi, 1)
                    hi(up1, 0, *units)

            up(up1, 0, t_up1, first)
            with act.Fori(1, NFF) as i:
                up(up1, i, t_up1, None)
            down(down1, t_up1)

            def conv_block(n):
                for t in range(TT):
                    act.wait_ge(tr_full, t_conv + 2 * n + t + 1)
                    act.activation(ch[:, BLK * n:BLK * (n + 1), PAD + t * P:PAD + (t + 1) * P],
                                   tb[:, t].rearrange("p (b n) -> p b n", b=BLK), ACT.Copy).then_inc(ch_ready, 1)

            def conv_gate(c, last):
                for t in range(TT):
                    tile_full(conv_in, 0, c, last, t)
                    act.activation(act_sb[:, t], acc[:, t], ACT.Sigmoid).then_inc(acc_out[0], 1)

            after_norm(conv_in, t_ln1)
            hi(conv_in, 0, 8, 9, 10, 11)
            conv_gate(0, UD - 1)
            hi(conv_in, 0, *range(12, 24))
            conv_block(0)
            hi(conv_in, 0, 24, 25, 26, 27)
            conv_gate(2, 3 * UD - 1)
            hi(conv_in, 0, 28, 29, 30, 31)
            hi(first_q, 0, *range(8))
            conv_block(1)

            with act.Fori(0, NG) as g:
                tg = TH * g + t_heads
                hi(heads, g, 0, 1, 2, 3)
                for t in range(TT):
                    if t == 0:
                        act.wait_ge(tile0_full, heads.chunk(g, 0))
                        act.wait_ge(tr_full, tg - TH + 4)
                    else:
                        act.wait_ge(unit_used, heads.unit(g, 0))
                    act.activation(act_sb[:, t], acc[:, t], ACT.Copy).then_inc(acc_out[0], 1)
                hi(heads, g, 4, 5, 6, 7)
                for t in range(TT):
                    act.wait_ge(tr_full, tg + (t + 1))
                    act.activation(qT[:, :, t * P:(t + 1) * P], tb[:, t].rearrange("p (b n) -> p b n", b=HG),
                                   ACT.Copy).then_inc(qk_ready, 1)
                hi(heads, g, 8, 9, 10, 11)
                for t in range(TT):
                    tile_full(heads, g, 0, UD - 1, t)
                    act.activation(act_sb[:, t], acc[:, 2 + t], ACT.Copy).then_inc(acc_out[1], 1)
                hi(heads, g, 12, 13, 14, 15)
                for t in range(TT):
                    act.wait_ge(tr_full, tg + (2 + t + 1))
                    act.activation(kT[:, :, t * P:(t + 1) * P], tb[:, 2 + t].rearrange("p (b n) -> p b n", b=HG),
                                   ACT.Copy).then_inc(qk_ready, 1)
                hi(heads, g, 16, 17, 18, 19)
                for t in range(TT):
                    tile_full(heads, g, 1, 2 * UD - 1, t)
                    act.activation(vt[:, t], acc[:, t], ACT.Copy).then_inc(acc_out[0], 1)
                hi(heads, g, 20, 21, 22, 23)
                act.wait_ge(smax_ready, 3 * g + 3)
                for h in range(HG):
                    for q, cols in enumerate((slice(0, P), slice(P, SC))):
                        n = HG * q + h
                        act.activation(pr[:, h, cols], pr[:, h, cols], ACT.Exp, bias=nmax[:, n:n + 1], scale=SCALE,
                                       accum_out=ssum[:, n:n + 1]).then_inc(exp_ready, 1)
                hi(heads, g, 24, 25, 26, 27)
                for t in range(TT):
                    tile_full(heads, g, 2, 3 * UD - 1, t)
                    act.activation(sig[:, bass.ds(g, 1), t], acc[:, 2 + t:3 + t], ACT.Sigmoid).then_inc(acc_out[1], 1)
                hi(heads, g, 28, 29, 30, 31)
                for h in range(HG):
                    act.wait_ge(tr_full, tg + (8 + h + 1))
                    act.activation(pT[:, h], tb[:, h, 0:SC], ACT.Copy).then_inc(pT_ready, 1)
                for b in range(2):
                    act.wait_ge(tr_full, tg + (12 + b + 1))
                    act.activation(oT_hi[:, bass.ds(4 * g + 2 * b, 2)],
                                   tb[:, b].rearrange("p (h n) -> p h n", h=2), ACT.Copy).then_inc(lhs_hi, 1)

            def conv_out_gate(i):
                for t in range(TT):
                    if t == 0:
                        act.wait_ge(tile0_full, gates.chunk(i - 1, 0))
                    else:
                        act.wait_ge(unit_used, gates.unit(i - 1, 0))
                    act.activation(sig[:, bass.ds(i + (ND - 1), 1), t], acc[:, t:t + 1],
                                   ACT.Sigmoid).then_inc(acc_out[0], 1)

            with act.Fori(1, ND) as i:
                hi(gates, i - 1, 0, 1, 2, 3)
                conv_out_gate(i)
                hi(gates, i - 1, 4, 5, 6, 7)

            hi(attn_out, 0, 0, 1, 2, 3)
            conv_out_gate(ND)
            hi(attn_out, 0, 4, 5, 6, 7)
            hi(attn_out, 1, 0, 1, 2, 3)
            for t in range(TT):
                act.wait_ge(ln_ready, 8 + t + 1)
                act.activation(ct[:, t], ct[:, t], ACT.Silu).then_inc(silu_ready, 1)
            hi(attn_out, 1, 4, 5, 6, 7)
            for t in range(TT):
                for half in range(2):
                    block_hi(cT_hi[:, BLK * half:BLK * (half + 1), t * P:(t + 1) * P], 2 * t + half,
                             t_convt + 2 * t + half + 1)
            with act.Fori(2, ND) as i:
                hi(attn_out, i, *range(UD))

            def merged_hi(c):
                for t in range(TT):
                    block_hi(oT_hi[:, BLK * c:BLK * (c + 1), t * P:(t + 1) * P], 2 * (c % 2) + t,
                             t_merge + 2 * c + t + 1)

            hi(conv_out, 0, *range(12))
            merged_hi(0)
            hi(conv_out, 0, 12, 13, 14, 15)
            merged_hi(1)

            hi(mix_out, 0, 0, 1, 2, 3)
            merged_hi(2)
            hi(mix_out, 0, 4, 5, 6, 7)
            merged_hi(3)
            with act.Fori(1, ND) as i:
                hi(mix_out, i, *range(UD))

            up(up2, 0, t_up2, lambda: after_norm(up2, t_ln2))
            with act.Fori(1, NFF) as i:
                up(up2, i, t_up2, None)
            down(down2, t_up2)

        @block.vector
        def _(dve):
            steps = [0]
            pieces_done = [0]

            def lo(seg, i, *units):
                for j in units:
                    dve.wait_ge(hi_ready, seg.unit(i, j) + 1)
                    s = seg.split(j)
                    dve.tensor_tensor(w_lo[:, s], raw[:, seg.raw(j)], f32(w_hi[:, s]),
                                      ALU.subtract).then_inc(lo_ready, 1)

            def tile_full(seg, i, c, last, t):
                if t == 0:
                    dve.wait_ge(tile0_full, seg.chunk(i, c) + 1)
                else:
                    dve.wait_ge(unit_used, seg.unit(i, last) + 1)

            def block_lo(dst, hi_part, bank, done):
                dve.wait_ge(lhs_hi, done)
                dve.tensor_tensor(dst, tb[:, bank].rearrange("p (b n) -> p b n", b=BLK), f32(hi_part),
                                  ALU.subtract).then_inc(lhs_lo, 1)

            def step(ins):
                ins.then_inc(ln_step, 1)
                steps[0] += 1
                return steps[0]

            def add_rows(t, cols, seg, i, uses):
                tile_full(seg, i, 0, seg.n - 1, t)
                dve.scalar_tensor_tensor(out=res[:, t, cols], in0=res[:, t, cols], scalar=ALPHA, in1=acc[:, t],
                                         op0=ALU.mult, op1=ALU.add).then_inc(acc_out[0], 1)

            def row_stats(t, c, cols, use):
                dve.wait_ge(acc_out[0], 2 * use + t + 1)
                return dve.bn_stats(stats[:, t, c], res[:, t, cols])

            def finish_stats(t, last, groups):
                dve.wait_ge(ln_step, step(last))
                done = step(dve.bn_aggr(mv[:, t], stats[:, t, 0:groups].rearrange("p a b -> p (a b)")))
                dve.wait_ge(ln_step, done)
                dve.tensor_scalar(var_eps[:, t], mv[:, t, 1:2], EPS, None, ALU.add).then_inc(var_ready, 1)

            def norm_pieces(t, pieces, gb):
                marks = []
                if pieces_done[0]:
                    dve.wait_ge(ln_ready, pieces_done[0])
                pieces_done[0] += len(pieces)
                for p in pieces:
                    cols = slice(p * COLS, (p + 1) * COLS)
                    marks.append(step(dve.scalar_tensor_tensor(
                        out=act_sb[:, p % 2], in0=res[:, t, cols], scalar=mv[:, t, 0:1], in1=gb[:, 0, cols],
                        op0=ALU.subtract, op1=ALU.mult)))
                for p, mark in zip(pieces, marks):
                    cols = slice(p * COLS, (p + 1) * COLS)
                    dve.wait_ge(ln_step, mark)
                    dve.scalar_tensor_tensor(out=res[:, t, cols], in0=act_sb[:, p % 2], scalar=rstd[:, t],
                                             in1=gb[:, 1, cols], op0=ALU.mult, op1=ALU.add).then_inc(ln_ready, 1)

            last_cols = slice((ND - 1) * COLS, D)

            def norm(seg, u0, n, b0, nxt):
                gb = ln_gb[n]
                use = u0 + ND - 1

                def piece_lo(m):
                    t, p = NORM_ORDER[m]
                    blocks, rows = slice(BLK * p, BLK * (p + 1)), slice(t * P, (t + 1) * P)
                    block_lo(xT_lo[:, blocks, rows], xT_hi[:, blocks, rows], 2 * t + p % 2, b0 + m + 1)

                lo(nxt, 0, 0, 1, 2, 3)
                add_rows(0, last_cols, seg, ND - 1, use)
                finish_stats(0, row_stats(0, ND - 1, last_cols, use), ND)
                dve.wait_ge(gb_loaded, 32 * (n + 1))
                dve.wait_ge(rstd_ready, rs[0] + 1)
                norm_pieces(0, (0, 1), gb)
                piece_lo(0)
                add_rows(1, last_cols, seg, ND - 1, use)
                finish_stats(1, row_stats(1, ND - 1, last_cols, use), ND)
                piece_lo(1)
                dve.wait_ge(rstd_ready, rs[0] + 2)
                norm_pieces(1, (0, 1), gb)
                piece_lo(2)
                norm_pieces(0, (2,), gb)
                piece_lo(3)
                lo(nxt, 0, 4)
                norm_pieces(0, (3,), gb)
                piece_lo(4)
                lo(nxt, 0, 5)
                piece_lo(5)
                lo(nxt, 0, 6)
                norm_pieces(1, (2,), gb)
                lo(nxt, 0, 7)
                norm_pieces(1, (3,), gb)
                piece_lo(6)
                piece_lo(7)
                rs[0] += 2

            rs = [0]

            def hidden(seg, i, last, use):
                for t in range(TT):
                    dve.wait_ge(acc_out[0], 2 * use + (t + 1))
                    tile_full(seg, i, 1, last, t)
                    dve.scalar_tensor_tensor(out=act_sb[:, t], in0=act_sb[:, t], scalar=0.5, in1=acc[:, 2 + t],
                                             op0=ALU.mult, op1=ALU.mult).then_inc(acc_out[1], 1)

            def hidden_lo(i, b0):
                for t in range(TT):
                    rows = slice(t * P, (t + 1) * P)
                    block_lo(hT_lo[:, bass.ds(BLK * i, BLK), rows], hT_hi[:, bass.ds(BLK * i, BLK), rows], t,
                              2 * i + (b0 + t + 1))

            def up(seg, u0, b0, start):
                start()
                lo(seg, 0, *range(8, 16))
                with dve.Fori(1, NFF) as i:
                    lo(seg, i, 0, 1, 2, 3)
                    hidden(seg, i - 1, 2 * UD - 1, i + (u0 - 1))
                    lo(seg, i, 4, 5, 6, 7)
                    hidden_lo(i - 1, b0)
                    lo(seg, i, *range(8, 16))

            def down(seg, before, u_up, u0, b0):
                lo(seg, 0, 0, 1, 2, 3)
                hidden(before, NFF - 1, 2 * UD - 1, u_up + NFF - 1)
                lo(seg, 0, 4, 5, 6, 7)
                hidden_lo(NFF - 1, b0)
                lo(seg, 0, *range(8, UF))
                with dve.Fori(1, ND) as i:
                    rows_before(seg, i, u0, lambda: lo(seg, i, 0, 1), lambda: lo(seg, i, 2, 3, 4))
                    lo(seg, i, *range(5, UF))

            def rows_before(seg, i, u0, ahead, between):
                cols = bass.ds(COLS * (i - 1), COLS)
                ahead()
                add_rows(0, cols, seg, i - 1, None)
                between()
                dve.wait_ge(acc_out[0], 2 * i + (2 * u0 - 1))
                dve.bn_stats(stats[:, 0, bass.ds(i - 1, 1)].rearrange("p a b -> p (a b)"), res[:, 0, cols])
                add_rows(1, cols, seg, i - 1, None)
                dve.wait_ge(acc_out[0], 2 * i + 2 * u0)
                dve.bn_stats(stats[:, 1, bass.ds(i - 1, 1)].rearrange("p a b -> p (a b)"), res[:, 1, cols])

            def first():
                for q, (blocks, units) in enumerate(START):
                    dve.wait_ge(lhs_hi, q + 1)
                    dve.tensor_tensor(xT_lo[:, blocks], x_stage[:, blocks], f32(xT_hi[:, blocks]),
                                      ALU.subtract).then_inc(lhs_lo, 1)
                    lo(up1, 0, *units)

            up(up1, 0, b_up1, first)
            dve.wait_ge(res_loaded, 16)
            down(down1, up1, 0, u0_down1, b_up1)
            norm(down1, u0_down1, 0, b_ln1, conv_in)

            def conv_value(c, last, use):
                for t in range(TT):
                    dve.wait_ge(acc_out[0], 2 * use + t + 1)
                    tile_full(conv_in, 0, c, last, t)
                    dve.tensor_tensor(act_sb[:, t], act_sb[:, t], acc[:, 2 + t], ALU.mult).then_inc(acc_out[1], 1)

            dve.memset(ch[:, :, 0:PAD], 0.0).then_inc(conv_step, 2)
            lo(conv_in, 0, *range(8, 20))
            conv_value(1, 2 * UD - 1, u0_conv)
            lo(conv_in, 0, *range(20, 32))
            lo(first_q, 0, 0, 1, 2, 3)
            conv_value(3, 4 * UD - 1, u0_conv + 1)
            lo(first_q, 0, 4, 5, 6, 7)
            dve.wait_ge(ch_ready, 4)
            dve.wait_ge(cw_loaded, 32)
            dve.wait_ge(alibi_loaded, 16)

            NT = 2 * TAPS
            with dve.Fori(0, NG) as g:
                tg = TH * g + t_heads

                def taps(first, count):
                    for n in range(first, min(first + count, NT)):
                        k, j = n % 2, n // 2
                        rows = ch[:, bass.ds(2 * g + k, 1), j:j + T].rearrange("p a n -> p (a n)")
                        w = cw[:, bass.ds(2 * TAPS * g + (k * TAPS + j), 1)]
                        dve.wait_ge(conv_step, NT * g + (n + 1))
                        if j == 0:
                            ins = dve.tensor_scalar(cacc[:, k], rows, w, cw[:, bass.ds(2 * g + (KC * TAPS + k), 1)],
                                                    ALU.mult, ALU.add)
                        else:
                            ins = dve.scalar_tensor_tensor(out=rows if j == TAPS - 1 else cacc[:, k], in0=rows,
                                                           scalar=w, in1=cacc[:, k], op0=ALU.mult, op1=ALU.add)
                        ins.then_inc(conv_step, 1)

                for j in range(20):
                    lo(heads, g, j)
                    taps(2 * j, 2)
                for h in range(HG):
                    dve.wait_ge(tr_full, tg + (4 + h + 1))
                    dve.scalar_tensor_tensor(out=pr[:, h], in0=alibi[:, 0:SC],
                                             scalar=alibi[:, bass.ds(HG * g + (SC + h), 1)],
                                             in1=tb[:, h, 0:SC], op0=ALU.mult, op1=ALU.add).then_inc(s_ready, 1)
                dve.wait_ge(s_ready, HG * g + HG)
                dve.tensor_reduce(smax[:, 0:HG], pr[:, :, 0:P], AX_X, ALU.max).then_inc(smax_ready, 1)
                dve.tensor_reduce(smax[:, HG:2 * HG], pr[:, :, P:SC], AX_X, ALU.max).then_inc(smax_ready, 1)
                dve.wait_ge(smax_ready, 3 * g + 2)
                dve.tensor_scalar(nmax[:], smax[:], -SCALE, None, ALU.mult).then_inc(smax_ready, 1)
                for j in range(20, 24):
                    lo(heads, g, j)
                    taps(2 * j, 2)
                lo(heads, g, 24)
                dve.wait_ge(exp_ready, 2 * HG * g + 2 * HG)
                dve.reciprocal(rsum[:], ssum[:]).then_inc(p_ready, 1)
                dve.wait_ge(p_ready, (2 * HG + 1) * g + 1)
                for h in range(HG):
                    for q, cols in enumerate((slice(0, P), slice(P, SC))):
                        n = HG * q + h
                        dve.tensor_scalar(pr[:, h, cols], pr[:, h, cols], rsum[:, n:n + 1], None,
                                          ALU.mult).then_inc(p_ready, 1)
                taps(48, 2)
                for j in range(25, 32):
                    lo(heads, g, j)
                    taps(2 * j, 2)
                for b in range(2):
                    two = bass.ds(4 * g + 2 * b, 2)
                    dve.wait_ge(lhs_hi, 2 * g + (b_heads + b + 1))
                    dve.tensor_tensor(oT_lo[:, two], tb[:, b].rearrange("p (h n) -> p h n", h=2), f32(oT_hi[:, two]),
                                      ALU.subtract).then_inc(lhs_lo, 1)

            with dve.Fori(0, ND - 1) as i:
                lo(gates, i, *range(UD))

            def attn_rows(i):
                for t in range(TT):
                    tile_full(attn_out, i - 1, 0, UD - 1, t)
                    g = sig[:, bass.ds(i - 1, 1), t]
                    dve.tensor_tensor(g, g, acc[:, 2 + t:3 + t], ALU.mult).then_inc(acc_out[1], 1)

            lo(attn_out, 0, 0, 1, 2, 3, 4, 5)
            dve.wait_ge(cgb_loaded, 32)
            for t in range(TT):
                lo(attn_out, 0, 6 + t)
                for half in range(2):
                    dve.wait_ge(tr_full, t_convo + 2 * t + half + 1)
                    last = dve.bn_stats(stats[:, t, half], tb[:, 2 * t + half])
                    if half == 0:
                        step(last)
                finish_stats(t, last, 2)
                dve.wait_ge(rstd_ready, rs[0] + 1 + t)
                marks = []
                for half in range(2):
                    cols = slice(half * COLS, (half + 1) * COLS)
                    marks.append(step(dve.scalar_tensor_tensor(
                        out=ct[:, t, cols], in0=tb[:, 2 * t + half], scalar=mv[:, t, 0:1], in1=cgb[:, 0, cols],
                        op0=ALU.subtract, op1=ALU.mult)))
                dve.wait_ge(ln_step, marks[-1])
                dve.scalar_tensor_tensor(out=ct[:, t], in0=ct[:, t], scalar=rstd[:, t], in1=cgb[:, 1],
                                         op0=ALU.mult, op1=ALU.add).then_inc(ln_ready, 1)
            rs[0] += 2
            pieces_done[0] += 2
            lo(attn_out, 1, 0, 1, 2, 3)
            attn_rows(1)
            lo(attn_out, 1, 4, 5, 6, 7)
            for t in range(TT):
                for half in range(2):
                    blocks, rows = slice(BLK * half, BLK * (half + 1)), slice(t * P, (t + 1) * P)
                    block_lo(cT_lo[:, blocks, rows], cT_hi[:, blocks, rows], 2 * t + half,
                              b_convt + 2 * t + half + 1)
            with dve.Fori(2, ND) as i:
                lo(attn_out, i, 0, 1, 2, 3)
                attn_rows(i)
                lo(attn_out, i, 4, 5, 6, 7)

            def merge(c):
                for t in range(TT):
                    tile_full(conv_out, 0, c, UC * (c + 1) - 1, t)
                    dve.tensor_tensor(sig[:, ND + c, t], sig[:, ND + c, t], acc[:, t], ALU.mult).then_inc(acc_out[0], 1)
                for t in range(TT):
                    dve.wait_ge(acc_out[0], 2 * (u0_convo + c) + t + 1)
                    dve.tensor_tensor(sig[:, c, t], sig[:, c, t], sig[:, ND + c, t], ALU.add).then_inc(merged, 1)

            def merged_lo(c):
                for t in range(TT):
                    blocks, rows = slice(BLK * c, BLK * (c + 1)), slice(t * P, (t + 1) * P)
                    block_lo(oT_lo[:, blocks, rows], oT_hi[:, blocks, rows], 2 * (c % 2) + t,
                              b_merge + 2 * c + t + 1)

            lo(conv_out, 0, 0, 1, 2, 3)
            attn_rows(ND)
            lo(conv_out, 0, 4, 5, 6, 7)
            merge(0)
            lo(conv_out, 0, 8, 9, 10, 11)
            merged_lo(0)
            merge(1)
            lo(conv_out, 0, 12, 13, 14, 15)
            merged_lo(1)
            merge(2)
            lo(mix_out, 0, 0, 1, 2, 3)
            merged_lo(2)
            merge(3)
            lo(mix_out, 0, 4, 5, 6, 7)
            merged_lo(3)
            with dve.Fori(1, ND) as i:
                rows_before(mix_out, i, u0_mix, lambda: lo(mix_out, i, 0, 1, 2, 3), lambda: None)
                lo(mix_out, i, 4, 5, 6, 7)

            up(up2, u0_up2, b_up2, lambda: norm(mix_out, u0_mix, 1, b_ln2, up2))
            down(down2, up2, u0_up2, u0_down2, b_up2)

            use = u0_down2 + ND - 1
            add_rows(0, last_cols, down2, ND - 1, use)
            finish_stats(0, row_stats(0, ND - 1, last_cols, use), ND)
            dve.wait_ge(gb_loaded, 96)
            dve.wait_ge(rstd_ready, rs[0] + 1)
            norm_pieces(0, (0, 1), ln_gb[2])
            add_rows(1, last_cols, down2, ND - 1, use)
            finish_stats(1, row_stats(1, ND - 1, last_cols, use), ND)
            norm_pieces(0, (2, 3), ln_gb[2])
            dve.wait_ge(rstd_ready, rs[0] + 2)
            norm_pieces(1, (0, 1), ln_gb[2])
            norm_pieces(1, (2, 3), ln_gb[2])

        @block.gpsimd
        def _(pool):
            nc.gpsimd.memset(minus_half[:], -0.5).then_inc(half_ready, 1)
            pool.wait_ge(half_ready, 1)
            for n in range(4 * TT):
                pool.wait_ge(var_ready, n + 1)
                nc.gpsimd.tensor_tensor(rstd[:, n % TT], var_eps[:, n % TT], minus_half[:],
                                        ALU.pow).then_inc(rstd_ready, 1)

        @block.tensor
        def _(pe):
            def product(out_ap, x, k, rows, s, b, begin, end):
                cols = slice(b * COLS, (b + 1) * COLS)
                pe.matmul(out_ap, x[0][:, k, rows], w_hi[:, s, cols], start=begin, stop=False)
                pe.matmul(out_ap, x[0][:, k, rows], w_lo[:, s, cols], start=False, stop=False)
                return pe.matmul(out_ap, x[1][:, k, rows], w_hi[:, s, cols], start=False, stop=end)

            def groups_of(n):
                size = (n - 1) % GROUP + 1
                return [range(0, size)] + [range(j, j + GROUP) for j in range(size, n, GROUP)]

            def chunk(seg, i, j0, n, pair, x, use, groups=None, after={}, ready={}):
                for units in groups or groups_of(n):
                    for t in range(TT):
                        rows = slice(t * P, (t + 1) * P)
                        if units[0] == 0:
                            v = 2 * use + (t - 1)
                            if not (isinstance(v, int) and v <= 0):
                                pe.wait_ge(acc_out[pair], v)
                        for j in units:
                            if t == 0:
                                pe.wait_ge(lo_ready, seg.unit(i, j0 + j) + 1)
                            if (j, t) in ready:
                                ready[(j, t)]()
                            for b in range(UK):
                                mm = product(acc[:, 2 * pair + t], x, UK * j + b, rows, seg.split(j0 + j), b,
                                             j == 0 and b == 0, j == n - 1 and b == UK - 1)
                            if t == 1:
                                mm.then_inc(unit_used, 1)
                            elif j == n - 1:
                                mm.then_inc(tile0_full, 1)
                            if (j, t) in after:
                                after[(j, t)]()

            def rows_out(seg, u0, x, behind_last, tail):
                g = groups_of(seg.n)
                with pe.Fori(1, ND) as i:
                    chunk(seg, i - 1, 0, seg.n, 0, x, i + (u0 - 1), groups=g[-tail:])
                    chunk(seg, i, 0, seg.n, 0, x, i + u0, groups=g[:-tail])
                chunk(seg, ND - 1, 0, seg.n, 0, x, u0 + ND - 1, groups=[range(g[-tail][0], seg.n)], after=behind_last)

            def turn(bank, blocks):
                for n, b in enumerate(blocks):
                    mm = pe.transpose(tb[:, bank, n * P:(n + 1) * P], b, ident[:])
                mm.then_inc(tr_full, 1)

            def turn_act(bank, t):
                turn(bank, [act_sb[:, t, n * P:(n + 1) * P] for n in range(BLK)])

            xT = (xT_hi, xT_lo)
            hT = (hT_hi, hT_lo)
            oT = (oT_hi, oT_lo)
            cT = (cT_hi, cT_lo)

            def wait_lhs(n):
                return lambda: pe.wait_ge(lhs_lo, n)

            def turn_hidden(i, u1, b0):
                for t in range(TT):
                    pe.wait_ge(acc_out[1], 2 * i + (2 * u1 + t + 1))
                    pe.wait_ge(lhs_lo, 2 * i + (b0 + t - 1))
                    turn_act(t, t)

            def up(seg, u0, u1, b0, after, ready):
                chunk(seg, 0, 0, UD, 0, xT, u0, after=after, ready=ready)
                chunk(seg, 0, UD, UD, 1, xT, u1)
                with pe.Fori(1, NFF) as i:
                    chunk(seg, i, 0, UD, 0, xT, i + u0, after={(3, 0): lambda: turn_hidden(i - 1, u1, b0)})
                    chunk(seg, i, UD, UD, 1, xT, i + u1)

            def down(seg, u0, u1, b0, behind_last, tail):
                chunk(seg, 0, 0, UF, 0, hT, u0, groups=groups_of(UF)[:-tail],
                      ready={(0, 0): wait_lhs(b0 + 2 * (NFF - 1))},
                      after={(groups_of(UF)[0][-1], 1): lambda: turn_hidden(NFF - 1, u1, b0)})
                pe.wait_ge(lhs_lo, b0 + 2 * NFF)
                rows_out(seg, u0, hT, behind_last, tail)

            def turn_piece(n, r0, b0):
                t, p = NORM_ORDER[n]
                pe.wait_ge(ln_ready, r0 + n + 1)
                pe.wait_ge(lhs_lo, b0 if n < 4 else b0 + n - 3)
                turn(2 * t + p % 2, [res[:, t, p * COLS + k * P:p * COLS + (k + 1) * P] for k in range(BLK)])

            def turns_before(seg, r0, b0):
                return {(seg.n - 2, 1): lambda: turn_piece(0, r0, b0), (seg.n - 1, 1): lambda: turn_piece(1, r0, b0)}

            def turns_behind(r0, b0):
                places = [(2, 0), (3, 0), (1, 1), (2, 1), (6, 0), (7, 0)]
                after = {at: (lambda n=n: turn_piece(n, r0, b0)) for n, at in enumerate(places, 2)}
                needed = [(0, 0), (2, 0), (0, 1), (2, 1), (4, 0), (6, 0), (4, 1), (6, 1)]
                return after, {at: wait_lhs(b0 + n + 1) for n, at in enumerate(needed)}

            up(up1, 0, 0, b_up1, {}, {(units[0], 0): wait_lhs(q + 1) for q, (_, units) in enumerate(START)})
            pe.wait_ge(ident_loaded, 16)
            down(down1, u0_down1, 0, b_up1, turns_before(down1, 0, b_ln1), 1)

            def turn_conv(n):
                for t in range(TT):
                    pe.wait_ge(acc_out[1], 2 * (NFF + n) + t + 1)
                    if n == 1:
                        pe.wait_ge(ch_ready, t + 1)
                    turn_act(t, t)

            after, ready = turns_behind(0, b_ln1)
            chunk(conv_in, 0, 0, UD, 0, xT, u0_conv, after=after, ready=ready)
            chunk(conv_in, 0, UD, UD, 1, xT, NFF)
            chunk(conv_in, 0, 2 * UD, UD, 0, xT, u0_conv + 1, after={(3, 0): lambda: turn_conv(0)})
            chunk(conv_in, 0, 3 * UD, UD, 1, xT, NFF + 1)
            chunk(first_q, 0, 0, UD, 0, xT, u0_q, after={(3, 0): lambda: turn_conv(1)})
            pe.wait_ge(ch_ready, 4)

            with pe.Fori(0, NG) as g:
                def turn_q():
                    for t in range(TT):
                        pe.wait_ge(acc_out[0], 2 * (2 * g) + (2 * u0_heads + t - 1))
                        pe.wait_ge(lhs_lo, 2 * g + b_heads)
                        turn_act(t, t)

                def turn_k():
                    for t in range(TT):
                        pe.wait_ge(acc_out[1], 2 * (2 * g) + (2 * u1_heads + t + 1))
                        turn_act(2 + t, t)

                def scores():
                    pe.wait_ge(qk_ready, 4 * g + 4)
                    for h in range(HG):
                        pe.matmul(tb[:, h, 0:P], qT[:, h, 0:P], kT[:, h, 0:P], start=True, stop=True)
                        pe.matmul(tb[:, h, P:SC], qT[:, h, P:T], kT[:, h, :], start=True,
                                  stop=True).then_inc(tr_full, 1)

                def turn_p():
                    pe.wait_ge(p_ready, (2 * HG + 1) * g + (2 * HG + 1))
                    for h in range(HG):
                        turn(h, [pr[:, h, n * P:(n + 1) * P] for n in range(3)])

                def outputs():
                    pe.wait_ge(pT_ready, HG * g + HG)
                    for h in range(HG):
                        o = tb[:, h // 2, (h % 2) * T:(h % 2 + 1) * T]
                        cols = slice(h * DH, (h + 1) * DH)
                        pe.matmul(o, vt[:, 0, cols], pT[:, h, 0:T], start=True, stop=False)
                        mm = pe.matmul(o[:, P:T], vt[:, 1, cols], pT[:, h, T:SC], start=False, stop=True)
                        if h % 2 == 1:
                            mm.then_inc(tr_full, 1)

                chunk(heads, g, 0, UD, 1, xT, 2 * g + u1_heads, after={(3, 0): turn_q})
                chunk(heads, g, UD, UD, 0, xT, 2 * g + u0_heads, after={(3, 0): turn_k, (7, 0): scores})
                chunk(heads, g, 2 * UD, UD, 1, xT, 2 * g + (u1_heads + 1))
                chunk(heads, g, 3 * UD, UD, 0, xT, 2 * g + (u0_heads + 1), after={(3, 0): turn_p, (3, 1): outputs})

            with pe.Fori(0, ND - 1) as i:
                chunk(gates, i, 0, UD, 0, xT, i + u0_gates)

            def turn_conv_out():
                pe.wait_ge(conv_step, 2 * TAPS * NG + 2)
                for t in range(TT):
                    for half in range(2):
                        turn(2 * t + half, [ch[:, BLK * half + n, PAD + t * P:PAD + (t + 1) * P] for n in range(BLK)])

            def turn_conv_rows():
                for t in range(TT):
                    pe.wait_ge(silu_ready, t + 1)
                    for half in range(2):
                        turn(2 * t + half, [ct[:, t, half * COLS + n * P:half * COLS + (n + 1) * P] for n in range(BLK)])

            chunk(attn_out, 0, 0, UD, 1, oT, u1_attn, ready={(0, 0): wait_lhs(b_convt)}, after={(3, 0): turn_conv_out})
            chunk(attn_out, 1, 0, UD, 1, oT, u1_attn + 1, after={(3, 0): turn_conv_rows})
            with pe.Fori(2, ND) as i:
                chunk(attn_out, i, 0, UD, 1, oT, i + u1_attn)

            def turn_merged(c):
                for t in range(TT):
                    pe.wait_ge(merged, 2 * c + t + 1)
                    if c >= 2:
                        pe.wait_ge(lhs_lo, b_merge + 2 * (c - 2) + t + 1)
                    turn(2 * (c % 2) + t, [sig[:, c, t, n * P:(n + 1) * P] for n in range(BLK)])

            for c in range(ND):
                chunk(conv_out, 0, c * UC, UC, 0, cT, u0_convo + c, ready={(0, 0): wait_lhs(b_merge)} if c == 0 else {},
                      after={(3, 0): lambda: turn_merged(c - 1)} if c else {})

            chunk(mix_out, 0, 0, UD, 0, oT, u0_mix, groups=groups_of(UD)[:1], ready={(0, 0): wait_lhs(b_merge + 4)},
                  after={(3, 0): lambda: turn_merged(ND - 1)})
            pe.wait_ge(lhs_lo, b_ln2)
            rows_out(mix_out, u0_mix, oT, turns_before(mix_out, 10, b_ln2), 1)

            after, ready = turns_behind(10, b_ln2)
            up(up2, u0_up2, u1_up2, b_up2, after, ready)
            down(down2, u0_down2, u1_up2, b_up2, {}, 2)


def units_of(w, col0):
    c = w[:, col0:col0 + COLS]
    return c.reshape(-1, UK, P, COLS).transpose(0, 2, 1, 3).reshape(-1, P, UNIT)


def weight_stream(i):
    q0, k0, v0, u0 = 0, D, 2 * D, 3 * D
    ga0, gc0 = 3 * D + 2 * CC, 4 * D + 2 * CC
    w_in = i["w_in"][0]
    parts = []

    def ffn(wg, wu, wd):
        for c in range(NFF):
            parts.extend([units_of(wg, c * COLS), units_of(wu, c * COLS)])
        parts.extend(units_of(wd, c * COLS) for c in range(ND))

    ffn(i["ffn1_wg"][0], i["ffn1_wu"][0], i["ffn1_wd"][0])
    for c in range(2):
        parts.extend([units_of(w_in, u0 + CC + c * COLS), units_of(w_in, u0 + c * COLS)])
    parts.append(units_of(w_in, q0))
    for g in range(NG):
        parts.extend([units_of(w_in, k0 + g * COLS), units_of(w_in, v0 + g * COLS), units_of(w_in, ga0 + g * COLS)])
        parts.append(units_of(w_in, q0 + (g + 1) * COLS if g + 1 < NG else gc0))
    parts.extend(units_of(w_in, gc0 + c * COLS) for c in range(1, ND))
    parts.extend(units_of(i["w_attn_out"][0], c * COLS) for c in range(ND))
    parts.extend(units_of(i["w_conv_out"][0], c * COLS) for c in range(ND))
    parts.extend(units_of(i["w_out"][0], c * COLS) for c in range(ND))
    ffn(i["ffn2_wg"][0], i["ffn2_wu"][0], i["ffn2_wd"][0])
    return np.concatenate(parts, axis=0)


def shape_constants():
    c = np.zeros((P, P + SC + H), np.float32)
    c[:, 0:P] = np.eye(P, dtype=np.float32)
    q = np.arange(P)[:, None]
    k = np.arange(P)[None, :]
    causal = np.where(k <= q, k - q, -1e37)
    c[:, P:P + SC] = np.concatenate([causal, k - (q + P), causal], axis=1)
    c[:, P + SC:] = [2.0 ** (-8.0 * (h + 1) / H) / SCALE for h in range(H)]
    return c


def kernel(**inputs):
    import concourse.bacc as _bacc
    from concourse.bass_utils import run_bass_kernel_spmd as _run

    i = {k: np.ascontiguousarray(v) for k, v in inputs.items()}
    x = i["x"][0]
    arrays = {
        "stream": weight_stream(i),
        "xT": np.ascontiguousarray(x.T.reshape(KD, P, T).transpose(1, 0, 2)),
        "x_rows": np.ascontiguousarray(x.reshape(TT, P, D).transpose(1, 0, 2)),
        "ln": np.concatenate([i[n] for n in ("ln1_g", "ln1_b", "ln2_g", "ln2_b", "ln3_g", "ln3_b")]),
        "conv_ln": np.concatenate([i["conv_ln_g"], i["conv_ln_b"]]),
        "conv_w": np.ascontiguousarray(i["conv_dw"][0, :, 0].reshape(TAPS, KC, P).transpose(2, 1, 0).reshape(P, -1)),
        "conv_b": np.ascontiguousarray(i["conv_db"][0].reshape(KC, P).T),
        "consts": shape_constants(),
    }
    nc = _bacc.Bacc("TRN2", target_bir_lowering=False, num_devices=1, dynamic_dma_scratch_size=1024)
    args = [nc.dram_tensor(f"in_{n}", a.shape, mybir.dt.from_np(a.dtype), kind="ExternalInput").ap()
            for n, a in arrays.items()]
    out = nc.dram_tensor("out_0", (T, D), F32, kind="ExternalOutput").ap()
    build(nc, *args, out)
    r = _run(nc, [{f"in_{n}": a for n, a in arrays.items()}], core_ids=[0])
    return r.results[0]["out_0"].reshape(1, T, D)
```
